# Optimizing a Trainium2 kernel written in Bass

```python
import numpy as np
import jax
import jax.numpy as jnp
from jax import lax

D_MODEL = 1024
BATCH = 1
SEQ = 256
DEPTH = 2
DEC_BATCH = 1
DEC_SEQ = 64
PAST_LEN = 512

CHUNK = 64
N_HEADS = 8
HEAD_DIM = 64
D_ATTN = N_HEADS * HEAD_DIM
IDX_HEADS = 8
IDX_DIM = 64
TOPK_MAX = 256
D_CONF = 512
CONF_WIDTH = 31
D_SC = 512
SC_WIDTH = 3
N_BRANCH = 3
D_BRANCH = 512
D_FF = 2816
N_EXPERTS = 8
TOP_K_EXPERTS = 2
D_FF_EXPERT = 1408
N_DENSE = (DEPTH + 1) // 2
N_MOE = DEPTH // 2
EPS = 1e-6
SPLIT_SIZES = (D_ATTN, HEAD_DIM, HEAD_DIM, IDX_HEADS * IDX_DIM, IDX_DIM, IDX_HEADS,
               2 * D_CONF, 3 * D_SC, N_BRANCH * D_MODEL)
D_IN = D_ATTN + 2 * HEAD_DIM + IDX_HEADS * IDX_DIM + IDX_DIM + IDX_HEADS + 2 * D_CONF + 3 * D_SC + N_BRANCH * D_MODEL

kernel_name = "streaming_hybrid_dsa_conformer_shortconv"

def _rmsnorm(x, g):
    xf = x.astype(jnp.float32)
    xf = xf * lax.rsqrt(jnp.mean(xf * xf, axis=-1, keepdims=True) + EPS)
    return xf.astype(x.dtype) * g

def _layernorm(x, g, b):
    xf = x.astype(jnp.float32)
    mu = jnp.mean(xf, axis=-1, keepdims=True)
    xc = xf - mu
    var = jnp.mean(xc * xc, axis=-1, keepdims=True)
    return (xc * lax.rsqrt(var + EPS)).astype(x.dtype) * g + b

def _dwconv_valid(xp, w):
    return lax.conv_general_dilated(
        xp, w.astype(xp.dtype)[:, None, :], window_strides=(1,), padding="VALID",
        dimension_numbers=("NWC", "WIO", "NWC"), feature_group_count=xp.shape[-1])

def _sparse_attend(q, iq, iw, k_all, v_all, ik_all, limit, topk):
    key_pos = jnp.arange(k_all.shape[1])
    rel = jax.nn.relu(jnp.einsum("bqhe,ble->bqhl", iq, ik_all).astype(jnp.float32) * IDX_DIM ** -0.5)
    score = jnp.einsum("bqh,bqhl->bql", iw.astype(jnp.float32) * IDX_HEADS ** -0.5, rel)
    score = jnp.where(key_pos < limit, score, -jnp.inf)
    _, sel = lax.top_k(score, topk)
    kv = jnp.concatenate([k_all, v_all], axis=-1)
    kv_sel = jax.vmap(lambda rows, ids: rows[ids])(kv, sel)
    k_sel, v_sel = jnp.split(kv_sel, 2, axis=-1)
    logits = jnp.einsum("bqhd,bqkd->bqhk", q, k_sel).astype(jnp.float32) * HEAD_DIM ** -0.5
    logits = jnp.where((sel < limit)[:, :, None, :], logits, -jnp.inf)
    p = jax.nn.softmax(logits, axis=-1).astype(v_sel.dtype)
    return jnp.einsum("bqhk,bqkd->bqhd", p, v_sel)

def _token_mixer(h, w_in, w_dw_conf, b_dw_conf, ln_conf_g, ln_conf_b, w_dw_short, w_branch, w_out, past):
    B, T, _ = h.shape
    offsets = np.cumsum(SPLIT_SIZES)[:-1].tolist()
    q, k, v, iq, ik, iw, glu, sc, gates = jnp.split(h @ w_in, offsets, axis=-1)
    q = q.reshape(B, T, N_HEADS, HEAD_DIM)
    iq = iq.reshape(B, T, IDX_HEADS, IDX_DIM)
    if past is None:
        n_blk = T // CHUNK
        topk = min(TOPK_MAX, T // 4)

        def blocks(a):
            return jnp.moveaxis(a.reshape((B, n_blk, CHUNK) + a.shape[2:]), 1, 0)

        def attend_block(args):
            qb, iqb, iwb, j = args
            return _sparse_attend(qb, iqb, iwb, k, v, ik, (j + 1) * CHUNK, topk)

        attn = lax.map(attend_block, (blocks(q), blocks(iq), blocks(iw), jnp.arange(n_blk)))
        attn = jnp.moveaxis(attn, 0, 1).reshape(B, T, D_ATTN)
        conf_hist = jnp.zeros((B, CONF_WIDTH - 1, D_CONF), h.dtype)
        short_hist = jnp.zeros((B, SC_WIDTH - 1, D_SC), h.dtype)
    else:
        cache_k, cache_v, cache_ik, conf_hist, short_hist = past
        k_all = jnp.concatenate([cache_k, k], axis=1)
        v_all = jnp.concatenate([cache_v, v], axis=1)
        ik_all = jnp.concatenate([cache_ik, ik], axis=1)
        n_keys = k_all.shape[1]
        attn = _sparse_attend(q, iq, iw, k_all, v_all, ik_all, n_keys,
                              min(TOPK_MAX, n_keys // 4)).reshape(B, T, D_ATTN)
    a, g = jnp.split(glu, 2, axis=-1)
    u_conf = jnp.concatenate([conf_hist, a * jax.nn.sigmoid(g)], axis=1)
    conv = _dwconv_valid(u_conf, w_dw_conf) + b_dw_conf
    conf = jax.nn.silu(_layernorm(conv, ln_conf_g, ln_conf_b))
    b_gate, c_gate, xs = jnp.split(sc, 3, axis=-1)
    u_short = jnp.concatenate([short_hist, c_gate * xs], axis=1)
    short = b_gate * _dwconv_valid(u_short, w_dw_short)
    g_a, g_b, g_c = jnp.split(jax.nn.sigmoid(gates), 3, axis=-1)
    merged = g_a * (attn @ w_branch[0]) + g_b * (conf @ w_branch[1]) + g_c * (short @ w_branch[2])
    out = merged @ w_out
    new_state = (k, v, ik, u_conf[:, -(CONF_WIDTH - 1):], u_short[:, -(SC_WIDTH - 1):])
    return out, new_state

def _swiglu(h, w_in, w_out):
    gate, up = jnp.split(h @ w_in, 2, axis=-1)
    return (jax.nn.silu(gate) * up) @ w_out

def _moe_swiglu(h, w_router, b_router, w_exp_in, w_exp_out):
    logits = (h @ w_router).astype(jnp.float32) + b_router
    top_val, top_idx = lax.top_k(logits, TOP_K_EXPERTS)
    top_w = jax.nn.softmax(top_val, axis=-1)
    combine = jnp.sum(jax.nn.one_hot(top_idx, N_EXPERTS, dtype=jnp.float32) * top_w[..., None], axis=-2)
    combine = combine.astype(h.dtype)
    out = jnp.zeros_like(h)
    for e in range(N_EXPERTS):
        out = out + combine[..., e:e + 1] * _swiglu(h, w_exp_in[e], w_exp_out[e])
    return out

def _trunk(x, c, past, p):
    c_act = jax.nn.silu(c)
    states = [[], [], [], [], []]
    for l in range(DEPTH):
        mod = (c_act @ p["w_ada"][l] + p["b_ada"][l])[:, None, :]
        shift_m, scale_m, gate_m, shift_f, scale_f, gate_f = jnp.split(mod, 6, axis=-1)
        h = _rmsnorm(x, p["g_norm_mix"][l]) * (1 + scale_m) + shift_m
        layer_past = None if past is None else (past[0][l], past[1][l], past[2][l], past[3][l], past[4][l])
        m, st = _token_mixer(h, p["w_in"][l], p["w_dw_conf"][l], p["b_dw_conf"][l], p["ln_conf_g"][l],
                             p["ln_conf_b"][l], p["w_dw_short"][l], p["w_branch"][l], p["w_out"][l], layer_past)
        for i in range(5):
            states[i].append(st[i])
        x = x + gate_m * m
        h = _rmsnorm(x, p["g_norm_ffn"][l]) * (1 + scale_f) + shift_f
        if l % 2 == 0:
            f = _swiglu(h, p["w_ffn_in"][l // 2], p["w_ffn_out"][l // 2])
        else:
            f = _moe_swiglu(h, p["w_router"][l // 2], p["b_router"][l // 2],
                            p["w_exp_in"][l // 2], p["w_exp_out"][l // 2])
        x = x + gate_f * f
    y = _rmsnorm(x, p["g_final"])
    return y, (jnp.stack(states[0]), jnp.stack(states[1]), jnp.stack(states[2]),
               jnp.stack(states[3]), jnp.stack(states[4]))

def setup_inputs(seed: int = 0) -> dict:
    key = jax.random.key(seed)
    ks = jax.random.split(key, 28)

    def nrm(k, shape, scale):
        return jax.random.normal(k, shape, jnp.float32) * scale

    return {
        "x_prompt": nrm(ks[0], (BATCH, SEQ, D_MODEL), 1.0),
        "x_sample": nrm(ks[1], (DEC_BATCH, DEC_SEQ, D_MODEL), 1.0),
        "cache_k": nrm(ks[2], (DEPTH, DEC_BATCH, PAST_LEN, HEAD_DIM), 1.0),
        "cache_v": nrm(ks[3], (DEPTH, DEC_BATCH, PAST_LEN, HEAD_DIM), 1.0),
        "cache_idx_k": nrm(ks[4], (DEPTH, DEC_BATCH, PAST_LEN, IDX_DIM), 1.0),
        "state_conv_conformer": nrm(ks[5], (DEPTH, DEC_BATCH, CONF_WIDTH - 1, D_CONF), 0.5),
        "state_conv_short": nrm(ks[6], (DEPTH, DEC_BATCH, SC_WIDTH - 1, D_SC), 1.0),
        "c_prompt": nrm(ks[7], (BATCH, D_MODEL), 1.0),
        "c_sample": nrm(ks[8], (DEC_BATCH, D_MODEL), 1.0),
        "w_ada": nrm(ks[9], (DEPTH, D_MODEL, 6 * D_MODEL), 0.3 * D_MODEL ** -0.5),
        "b_ada": nrm(ks[10], (DEPTH, 6 * D_MODEL), 0.02),
        "g_norm_mix": 1.0 + nrm(ks[11], (DEPTH, D_MODEL), 0.02),
        "g_norm_ffn": 1.0 + nrm(ks[12], (DEPTH, D_MODEL), 0.02),
        "w_in": nrm(ks[13], (DEPTH, D_MODEL, D_IN), D_MODEL ** -0.5),
        "w_dw_conf": nrm(ks[14], (DEPTH, CONF_WIDTH, D_CONF), CONF_WIDTH ** -0.5),
        "b_dw_conf": nrm(ks[15], (DEPTH, D_CONF), 0.02),
        "ln_conf_g": 1.0 + nrm(ks[16], (DEPTH, D_CONF), 0.02),
        "ln_conf_b": nrm(ks[17], (DEPTH, D_CONF), 0.02),
        "w_dw_short": nrm(ks[18], (DEPTH, SC_WIDTH, D_SC), SC_WIDTH ** -0.5),
        "w_branch": nrm(ks[19], (DEPTH, N_BRANCH, D_BRANCH, D_MODEL), D_BRANCH ** -0.5),
        "w_out": nrm(ks[20], (DEPTH, D_MODEL, D_MODEL), D_MODEL ** -0.5),
        "w_ffn_in": nrm(ks[21], (N_DENSE, D_MODEL, 2 * D_FF), D_MODEL ** -0.5),
        "w_ffn_out": nrm(ks[22], (N_DENSE, D_FF, D_MODEL), D_FF ** -0.5),
        "w_router": nrm(ks[23], (N_MOE, D_MODEL, N_EXPERTS), D_MODEL ** -0.5),
        "b_router": nrm(ks[24], (N_MOE, N_EXPERTS), 0.01),
        "w_exp_in": nrm(ks[25], (N_MOE, N_EXPERTS, D_MODEL, 2 * D_FF_EXPERT), D_MODEL ** -0.5),
        "w_exp_out": nrm(ks[26], (N_MOE, N_EXPERTS, D_FF_EXPERT, D_MODEL), D_FF_EXPERT ** -0.5),
        "g_final": 1.0 + nrm(ks[27], (D_MODEL,), 0.02),
    }

def reference(x_prompt, x_sample, cache_k, cache_v, cache_idx_k, state_conv_conformer, state_conv_short,
              c_prompt, c_sample, w_ada, b_ada, g_norm_mix, g_norm_ffn, w_in, w_dw_conf, b_dw_conf,
              ln_conf_g, ln_conf_b, w_dw_short, w_branch, w_out, w_ffn_in, w_ffn_out, w_router, b_router,
              w_exp_in, w_exp_out, g_final):
    params = {
        "w_ada": w_ada, "b_ada": b_ada, "g_norm_mix": g_norm_mix, "g_norm_ffn": g_norm_ffn,
        "w_in": w_in, "w_dw_conf": w_dw_conf, "b_dw_conf": b_dw_conf, "ln_conf_g": ln_conf_g,
        "ln_conf_b": ln_conf_b, "w_dw_short": w_dw_short, "w_branch": w_branch, "w_out": w_out,
        "w_ffn_in": w_ffn_in, "w_ffn_out": w_ffn_out, "w_router": w_router, "b_router": b_router,
        "w_exp_in": w_exp_in, "w_exp_out": w_exp_out, "g_final": g_final,
    }
    y_prompt, (pk, pv, pik, pconf, pshort) = _trunk(x_prompt, c_prompt, None, params)
    y_sample, (sk, sv, sik, sconf, sshort) = _trunk(
        x_sample, c_sample, (cache_k, cache_v, cache_idx_k, state_conv_conformer, state_conv_short), params)
    return (y_prompt, y_sample, pk, pv, pik, pconf, pshort, sk, sv, sik, sconf, sshort)


_drawn_inputs = setup_inputs


def setup_inputs(seed=0):
    import zlib

    import numpy as np

    out = dict(_drawn_inputs(seed))
    spreads = {}
    factors = {'cache_k': 3.998,
     'cache_v': 3.098,
     'cache_idx_k': 3.406,
     'state_conv_short': 3.196,
     'g_norm_ffn': 6.129,
     'b_dw_conf': 8.0,
     'ln_conf_g': 8.0,
     'ln_conf_b': 8.0,
     'b_router': 8.0,
     'g_final': 3.099}
    for name, (base, spread) in spreads.items():
        noise = np.random.default_rng([zlib.crc32(name.encode()), seed]).standard_normal(out[name].shape)
        drawn = base * np.exp(spread * noise) if base else spread * noise
        out[name] = jnp.asarray(drawn.astype(out[name].dtype))
    for name, factor in factors.items():
        out[name] = (out[name] * factor).astype(out[name].dtype)
    return out
```

```python
from contextlib import ExitStack

import numpy as np

import concourse.bass as bass
from concourse import mybir

F32 = mybir.dt.float32
U32 = mybir.dt.uint32
I32 = mybir.dt.int32
ALU = mybir.AluOpType
ACT = mybir.ActivationFunctionType
AX = mybir.AxisListType.X

P = 128
D = 1024
DC = D // P
TP, TS = 256, 64
T = TP + TS
TW = T + TS
DEPTH = 2
PAST = 512
NKS = PAST + TS
CHUNK = 64
NH, HD = 8, 64
DA = NH * HD
TOPK_P = min(256, TP // 4)
TOPK_S = min(256, NKS // 4)
DB = 512
BC = DB // P
CW, SW = 31, 3
DFF, DFE, NE = 2816, 1408, 8
FC, EC = DFF // P, DFE // P
EPS = 1e-6

Q0 = 0
K0 = Q0 + DA
V0 = K0 + HD
IQ0 = V0 + HD
IK0 = IQ0 + DA
IW0 = IK0 + HD
GLU0 = IW0 + NH
SC0 = GLU0 + 2 * DB
GATE0 = SC0 + 3 * DB

NEG_MASK = -1e30
INADMISSIBLE = -1e38
TAKEN = float(np.float32(-3e38))

CH, SH = CW - 1, SW - 1
UCW = 2 * CH + T
USW = 2 * SH + T
UC_P, UC_S = CH, 2 * CH + TP
US_P, US_S = SH, 2 * SH + TP

R_BADA, R_GMIX, R_GFFN, R_BDW, R_LNG, R_LNB, R_WSH, R_GFIN, R_C = 0, 48, 56, 64, 68, 72, 76, 88, 96
NROWS = 112

SLOTS = 4
SLOT = 2 * EC * P
NUNITS = 12


def plan():
    first, tmp, n, t = {}, {}, 0, 0
    stages = [("ada", 0, 24, 0), ("ada", 1, 24, 0)]
    for l in range(DEPTH):
        stages += [("qkv", l, 7, 0), ("glu", l, 4, 1), ("cxs", l, 4, 1), ("bgate", l, 2, 0), ("gates", l, 12, 0),
                   ("short", l, 4, 1), ("attn", l, 4, 1), ("conf", l, 4, 1), ("out", l, 4, 1)]
        if l % 2 == 0:
            stages += [("ffn_in", l, FC, 1), ("ffn_out", l, DC, 1)]
        else:
            stages += [("moe", l, 16, 1)]
    for name, l, count, uses_tmp in stages:
        first[name, l], tmp[name, l] = n, t
        n += count
        t += count * uses_tmp
    return first, tmp


def build(nc, x_prompt, x_sample, cache_k, cache_v, cache_idx_k, state_conv_conformer, state_conv_short,
          c_prompt, c_sample, w_ada, b_ada, g_norm_mix, g_norm_ffn, w_in, w_dw_conf, b_dw_conf,
          ln_conf_g, ln_conf_b, w_dw_short, w_branch, w_out, w_ffn_in, w_ffn_out, w_router, b_router,
          w_exp_in, w_exp_out, g_final,
          y_prompt, y_sample, pk, pv, pik, pconf, pshort, sk, sv, sik, sconf, sshort):
    first, tmp_before = plan()
    ADA_CHUNKS = 2 * 24

    with ExitStack() as ctx:
        def sb(name, shape, dt=F32):
            return ctx.enter_context(nc.sbuf_tensor(name, shape, dt))

        def sem(name):
            return ctx.enter_context(nc.semaphore(name))

        xT = sb("xT", [P, DC, T])
        hT = sb("hT", [P, DC, T])
        tok = sb("tok", [P, 3 * D])
        ring = sb("ring", [P, SLOTS, SLOT])
        wide = sb("wide", [P, 3 * DC, T])
        qT = sb("qT", [P, 4, T])
        iqT = sb("iqT", [P, 4, TW])
        kT = sb("kT", [P, TW])
        ikT = sb("ikT", [P, TW])
        viwT = sb("viwT", [P, TW])
        kTs = sb("kTs", [P, DEPTH, NKS])
        ikTs = sb("ikTs", [P, DEPTH, NKS])
        cv = sb("cv", [P, DEPTH, PAST // P, HD])
        u_conf = sb("u_conf", [P, BC, UCW])
        conv = sb("conv", [P, BC, UCW - CH])
        u_short = sb("u_short", [P, BC, USW])
        sconv = sb("sconv", [P, BC, USW - SH])
        bgate = sb("bgate", [P, BC, T])
        merged = sb("merged", [P, DC, T])
        score = sb("score", [P, 960])
        work = sb("work", [P, 960])
        lm = sb("lm", [P, NKS])
        prob = sb("prob", [P, NKS])
        probT = sb("probT", [P, 2, 640])
        tmp = sb("tmp", [P, 2, 2, T])
        mean = sb("mean", [P, T])
        var = sb("var", [P, T])
        std = sb("std", [P, T])
        rstd = sb("rstd", [P, T])
        vec = sb("vec", [P, DEPTH, NROWS])
        dwc = sb("dwc", [P, DEPTH, CW * BC])
        cT = sb("cT", [P, DC, 2])
        mods = sb("mods", [P, DEPTH, 48, 2])
        gain = sb("gain", [P, DEPTH, 2, DC, 2])
        hist = sb("hist", [P, DEPTH, BC, CH + SH])
        ident = sb("ident", [P, P])
        ones = sb("ones", [P, P])
        top8 = sb("top8", [P, 8])
        iws = sb("iws", [P, 3, NH])
        nmax = sb("nmax", [P, 2])
        psums = sb("psums", [P, 2])
        prec = sb("prec", [P, 2])
        wr = sb("wr", [P, DC, NE])
        br = sb("br", [1, NE])
        iota_i = sb("iota_i", [P, NE], I32)
        iota_f = sb("iota_f", [P, NE])
        idx_u = sb("idx_u", [P, 8], U32)
        idx_f = sb("idx_f", [P, 8])
        rl = sb("rl", [P, 3, NE])
        comb = sb("comb", [P, 3, NE])
        comb2 = sb("comb2", [P, NE])
        rsc = sb("rsc", [P, 8])

        x_tok = tok[:, :].rearrange("p (t d) -> p t d", t=3)
        st_out = tok[:, 0:4 * DB].rearrange("p (s d) -> p s d", s=4)
        kvtok = tok[:, 4 * DB:4 * DB + 3 * 328].rearrange("p (t d) -> p t d", t=3)
        comb_bc = tok[:, 0:NE * T].rearrange("p (e t) -> p e t", e=NE)
        wide_flat = wide[:, :, :].rearrange("p a b -> p (a b)")
        vrows = wide_flat[:, 0:DEPTH * 256].rearrange("p (l m c) -> p l m c", l=DEPTH, m=2)
        craw = wide_flat[:, 512:512 + DEPTH * 1024].rearrange("p (l m k c) -> p l m k c", l=DEPTH, m=2, k=4)
        hraw = wide_flat[:, 2560:2560 + DEPTH * 1024].rearrange("p (l m c) -> p l m c", l=DEPTH, m=2)
        gates = wide
        hid = wide
        attnT = iqT[:, :, 0:T]
        confT = qT
        shortT = u_short[:, :, :].rearrange("p a b -> p (a b)")[:, 0:BC * T].rearrange("p (a b) -> p a b", a=BC)
        rel = merged[:, :, :].rearrange("p a b -> p (a b)")[:, 0:1920].rearrange("p (a b) -> p a b", a=2)
        sq = merged
        acc = merged

        mmp = ctx.enter_context(nc.psum_tensor("mmp", [P, 4, 512], F32))
        lg = ctx.enter_context(nc.psum_tensor("lg", [P, 1024], F32))
        px = ctx.enter_context(nc.psum_tensor("px", [P, 512], F32))
        py = ctx.enter_context(nc.psum_tensor("py", [P, 512], F32))

        consts_ready = sem("consts_ready")
        w_full = [sem(f"w_full{i}") for i in range(SLOTS)]
        chunk_done = sem("chunk_done")
        pair_evac = sem("pair_evac")
        tmp_ready = sem("tmp_ready")
        tmp_free = sem("tmp_free")
        rows_loaded = sem("rows_loaded")
        x_loaded = sem("x_loaded")
        caches_loaded = sem("caches_loaded")
        router_loaded = sem("router_loaded")
        pro_tr = sem("pro_tr")
        pro_copied = sem("pro_copied")
        c_ready = sem("c_ready")
        mods_ready = sem("mods_ready")
        x_ready = sem("x_ready")
        sq_ready = sem("sq_ready")
        sum_ready = sem("sum_ready")
        ms_ready = sem("ms_ready")
        std_ready = sem("std_ready")
        xn_ready = sem("xn_ready")
        h_ready = sem("h_ready")
        kv_tr = sem("kv_tr")
        kv_copied = sem("kv_copied")
        sc_done = sem("sc_done")
        rel_ready = sem("rel_ready")
        rel_used = sem("rel_used")
        hist_ready = sem("hist_ready")
        u_ready = sem("u_ready")
        st_tr = sem("st_tr")
        st_copied = sem("st_copied")
        stored = sem("stored")
        lg_done = sem("lg_done")
        lm_done = sem("lm_done")
        exp_done = sem("exp_done")
        prob_ready = sem("prob_ready")
        pt_done = sem("pt_done")
        pt_copied = sem("pt_copied")
        av_done = sem("av_done")
        attn_copied = sem("attn_copied")
        short_ready = sem("short_ready")
        conv_ready = sem("conv_ready")
        ln_sum = sem("ln_sum")
        xc_ready = sem("xc_ready")
        ln_sq = sem("ln_sq")
        ln_ss = sem("ln_ss")
        ln_ms = sem("ln_ms")
        ln_std = sem("ln_std")
        ln_n = sem("ln_n")
        conf_ready = sem("conf_ready")
        merged_ready = sem("merged_ready")
        hid_ready = sem("hid_ready")
        rt_done = sem("rt_done")
        rt_d = sem("rt_d")
        rt_e = sem("rt_e")
        comb_ready = sem("comb_ready")
        cb_done = sem("cb_done")
        cb_copied = sem("cb_copied")
        y_ready = sem("y_ready")
        y_tr = sem("y_tr")
        y_copied = sem("y_copied")
        y_stored = sem("y_stored")
        dve_step = sem("dve_step")
        pool_step = sem("pool_step")

        w3 = {"in": w_in.rearrange("l (c p) n -> l p c n", p=P),
              "ada": w_ada.rearrange("l (c p) n -> l p c n", p=P),
              "out": w_out.rearrange("l (c p) n -> l p c n", p=P),
              "branch": w_branch.rearrange("l b (c p) n -> l b p c n", p=P),
              "ffn_in": w_ffn_in.rearrange("l (c p) n -> l p c n", p=P),
              "ffn_out": w_ffn_out.rearrange("l (c p) n -> l p c n", p=P),
              "exp_in": w_exp_in.rearrange("l e (c p) n -> l e p c n", p=P),
              "exp_out": w_exp_out.rearrange("l e (c p) n -> l e p c n", p=P)}

        def slot_view(slot, k, n):
            return ring[:, slot, 0:k * n].rearrange("p (k n) -> p k n", k=k)

        def segs(buf, off_p, off_s):
            return [(buf[..., off_p:off_p + TP], slice(0, TP)), (buf[..., off_s:off_s + TS], slice(TP, T))]

        block = ctx.enter_context(nc.Block())

        @block.sync
        def _(sp):
            def load(n, parts, it=None, per=SLOTS):
                if it is not None:
                    sp.wait_ge(chunk_done, it * per + (n - SLOTS + 1))
                elif n >= SLOTS:
                    sp.wait_ge(chunk_done, n - SLOTS + 1)
                assert len(parts) == 2
                for dst, src in parts:
                    sp.dma_start(dst, src).then_inc(w_full[n % SLOTS], 16)

            def halves(v, src, k):
                return [(v[:, 0:k // 2], src[:, 0:k // 2]), (v[:, k // 2:k], src[:, k // 2:k])]

            def cols(n, src, c0, k=DC, width=2 * P):
                return halves(slot_view(n % SLOTS, k, width), src[:, :, c0:c0 + width], k)

            def two_blocks(n, src, ca, cb, k=DC):
                v = slot_view(n % SLOTS, k, 2 * P)
                return [(v[:, :, 0:P], src[:, :, ca:ca + P]), (v[:, :, P:2 * P], src[:, :, cb:cb + P])]

            def dyn_cols(n, src, expr, k=DC, width=2 * P):
                return halves(slot_view(n % SLOTS, k, width), src[:, :, bass.ds(expr, width)], k)

            def dyn_two(n, src, expr, gap, k=DC):
                v = slot_view(n % SLOTS, k, 2 * P)
                return [(v[:, :, 0:P], src[:, :, bass.ds(expr, P)]), (v[:, :, P:2 * P], src[:, :, bass.ds(expr + gap, P)])]

            for l in range(DEPTH):
                n0 = first["ada", l]
                peel = SLOTS if l == 0 else 0
                for k in range(peel):
                    load(n0 + k, cols(n0 + k, w3["ada"][l], 2 * P * k))
                with sp.Fori(0, 24 // SLOTS - peel // SLOTS) as it:
                    for k in range(SLOTS):
                        n = n0 + peel + k
                        load(n, dyn_cols(n, w3["ada"][l], it * (SLOTS * 2 * P) + 2 * P * (k + peel)), it)

            for l in range(DEPTH):
                win = w3["in"][l]
                n = first["qkv", l]
                for i, c in enumerate((K0, IK0)):
                    v = slot_view((n + i) % SLOTS, DC, P)
                    load(n + i, [(v[:, :, r * HD:(r + 1) * HD], win[:, :, c:c + HD]) for r in range(2)])
                n += 1
                load(n + 1, cols(n + 1, win, IQ0))
                load(n + 2, cols(n + 2, win, IQ0 + 2 * P))
                v = slot_view((n + 3) % SLOTS, DC, 2 * P)
                load(n + 3, [(v[:, :, 0:HD], win[:, :, V0:V0 + HD]), (v[:, :, HD:HD + NH], win[:, :, IW0:IW0 + NH])])
                load(n + 4, cols(n + 4, win, Q0))
                load(n + 5, cols(n + 5, win, Q0 + 2 * P))
                for j in range(BC):
                    n = first["glu", l] + j
                    load(n, two_blocks(n, win, GLU0 + P * j, GLU0 + DB + P * j))
                for j in range(BC):
                    n = first["cxs", l] + j
                    load(n, two_blocks(n, win, SC0 + DB + P * j, SC0 + 2 * DB + P * j))
                for j in range(2):
                    n = first["bgate", l] + j
                    load(n, cols(n, win, SC0 + 2 * P * j))
                for j in range(12):
                    n = first["gates", l] + j
                    load(n, cols(n, win, GATE0 + 2 * P * j))
                for stage, b in (("short", 2), ("attn", 0), ("conf", 1)):
                    for j in range(4):
                        n = first[stage, l] + j
                        load(n, cols(n, w3["branch"][l, b], 2 * P * j, BC))
                for j in range(4):
                    n = first["out", l] + j
                    load(n, cols(n, w3["out"][l], 2 * P * j))
                if l % 2 == 0:
                    n0 = first["ffn_in", l]
                    with sp.Fori(0, FC // SLOTS) as it:
                        for k in range(SLOTS):
                            load(n0 + k, dyn_two(n0 + k, w3["ffn_in"][l // 2], it * (SLOTS * P) + P * k, DFF), it)
                    for k in range(FC - FC % SLOTS, FC):
                        load(n0 + k, two_blocks(n0 + k, w3["ffn_in"][l // 2], P * k, DFF + P * k))
                    n0 = first["ffn_out", l]
                    with sp.Fori(0, DC // SLOTS) as it:
                        for k in range(SLOTS):
                            load(n0 + k, dyn_cols(n0 + k, w3["ffn_out"][l // 2], it * (SLOTS * P) + P * k, FC, P), it)
                else:
                    n0 = first["moe", l]
                    with sp.Fori(0, NE) as e:
                        win_e = w3["exp_in"][l // 2, bass.ds(e, 1)].rearrange("e p c n -> (e p) c n")
                        wout_e = w3["exp_out"][l // 2, bass.ds(e, 1)].rearrange("e p c n -> (e p) c n")
                        for k in range(EC):
                            load(n0 + k, two_blocks(n0 + k, win_e, P * k, DFE + P * k), e, 16)
                        for k in range(4):
                            n = n0 + EC + k
                            load(n, cols(n, wout_e, 2 * P * k, EC), e, 16)

        @block.gpsimd
        def _(pool):
            nc.gpsimd.memset(ident[:], 0.0).then_inc(pool_step, 1)
            nc.gpsimd.memset(ones[:], 1.0).then_inc(consts_ready, 1)
            nc.gpsimd.memset(u_conf[:, :, 0:CH], 0.0).then_inc(consts_ready, 1)
            nc.gpsimd.iota(iota_i[:], pattern=[[1, NE]], base=0, channel_multiplier=0).then_inc(pool_step, 1)
            pool.wait_ge(pool_step, 2)
            nc.gpsimd.tensor_copy(iota_f[:], iota_i[:]).then_inc(consts_ready, 1)
            nc.gpsimd.affine_select(out=ident[:], in_=ident[:], compare_op=ALU.not_equal, fill=1.0, base=0,
                                    pattern=[[-1, P]], channel_multiplier=1).then_inc(consts_ready, 1)

            for l in range(DEPTH):
                pool.wait_ge(pro_copied, 14)
                if l > 0:
                    pool.wait_ge(x_ready, 2 * l + 1)
                nc.gpsimd.memset(u_short[:, :, 0:SH], 0.0)
                nc.gpsimd.tensor_copy(u_conf[:, :, CH + TP:2 * CH + TP], hist[:, l, :, 0:CH])
                nc.gpsimd.tensor_copy(u_short[:, :, SH + TP:2 * SH + TP],
                                      hist[:, l, :, CH:CH + SH]).then_inc(hist_ready, 1)
                for stage, buf, op, os in (("glu", u_conf, UC_P, UC_S), ("cxs", u_short, US_P, US_S)):
                    for j in range(BC):
                        t = tmp_before[stage, l] + j
                        pool.wait_ge(tmp_ready, t + 1)
                        for dst, s in segs(buf[:, j, :], op, os):
                            ins = nc.gpsimd.tensor_tensor(dst, tmp[:, t % 2, 0, s], tmp[:, t % 2, 1, s], ALU.mult)
                        ins.then_inc(u_ready, 1)
                        pool.wait_ge(u_ready, 8 * l + 4 * (stage == "cxs") + j + 1)
                        nc.gpsimd.sem_inc(tmp_free, 1)

        @block.tensor
        def _(pe):
            def group(out, pairs, **kw):
                for i, (a, b) in enumerate(pairs):
                    ins = nc.tensor.matmul(out, a, b, start=(i == 0), stop=(i == len(pairs) - 1), **kw)
                return ins

            def w_wait(n, it=None):
                if it is None:
                    pe.wait_ge(w_full[n % SLOTS], 32 * (n // SLOTS + 1))
                else:
                    pe.wait_ge(w_full[n % SLOTS], it * 32 + 32 * (n // SLOTS + 1))

            def pair_wait(n, it=None, per=SLOTS):
                need = n - ADA_CHUNKS - 1
                if it is not None:
                    pe.wait_ge(pair_evac, it * per + need)
                elif need >= 1:
                    pe.wait_ge(pair_evac, need)

            def pair_chunk(n, rhs, k=DC, blocks=((0, P), (P, P)), it=None, each=None, width=2 * P):
                w_wait(n, it)
                pair_wait(n, it)
                v = slot_view(n % SLOTS, k, width)
                for b, (c0, m) in enumerate(blocks):
                    for i in range(k):
                        if each is not None and b == 0:
                            each(i)
                        ins = nc.tensor.matmul(mmp[0:m, 2 * (n % 2) + b, 0:T], v[:, i, c0:c0 + m], rhs(i),
                                               start=(i == 0), stop=(i == k - 1))
                ins.then_inc(chunk_done, 1)

            def norm_sums(k):
                pe.wait_ge(sq_ready, k + 1)
                group(py[:, 0:T], [(ones[:], sq[:, c, :]) for c in range(DC)]).then_inc(sum_ready, 1)

            def h_rhs(i):
                return hT[:, i, :]

            def h_each(k):
                return lambda i: pe.wait_ge(h_ready, DC * k + i + 1)

            batch = [0]

            def pro(trs):
                b = batch[0]
                batch[0] += 1
                if b >= 4:
                    pe.wait_ge(pro_copied, b - 3)
                for out, in_, k in trs(mmp[:, b % 4, :]):
                    ins = nc.tensor.transpose(out, in_, ident[0:k, 0:k])
                ins.then_inc(pro_tr, 1)

            pe.wait_ge(consts_ready, 4)
            pe.wait_ge(rows_loaded, 16 * 26)
            for l in range(DEPTH):
                pro(lambda b: [(b[:, 0:NROWS], vrows[0:NROWS, l, 0, :], NROWS),
                               (b[:, P:P + CW * BC], vrows[0:CW * BC, l, 1, :], CW * BC)])
            pe.wait_ge(x_loaded, 32)
            for t in range(3):
                m = P if t < 2 else TS
                for g in range(2):
                    pro(lambda b: [(b[:, j * P:j * P + m], x_tok[0:m, t, (4 * g + j) * P:(4 * g + j + 1) * P], m)
                                   for j in range(4)])
            pe.wait_ge(caches_loaded, 16 * 14)
            for l in range(DEPTH):
                for m in range(2):
                    pro(lambda b: [(b[:, j * P:(j + 1) * P], craw[:, l, m, j, :], P) for j in range(4)])
                pro(lambda b: [(b[:, j * 32:j * 32 + CH], hraw[0:CH, l, 0, j * P:(j + 1) * P], CH) for j in range(4)]
                    + [(b[:, j * 32 + CH:j * 32 + 32], hraw[0:SH, l, 1, j * P:(j + 1) * P], SH) for j in range(4)])

            pe.wait_ge(c_ready, 1)

            def ada_chunk(n, out, it):
                w_wait(n, it)
                v = slot_view(n % SLOTS, DC, 2 * P)
                for b in range(2):
                    ins = group(out(b), [(v[:, i, b * P:(b + 1) * P], cT[:, i, :]) for i in range(DC)])
                ins.then_inc(chunk_done, 1)

            for l in range(DEPTH):
                acc_bank = (px, py)[l]
                n0 = first["ada", l]
                with pe.Fori(0, 24 // SLOTS) as it:
                    for k in range(SLOTS):
                        ada_chunk(n0 + k, lambda b: acc_bank[:, bass.ds(it * (4 * SLOTS) + (4 * k + 2 * b), 2)], it)

            for l in range(DEPTH):
                norm_sums(2 * l)
                n = first["qkv", l]
                pair_chunk(n, h_rhs, blocks=((0, P),), width=P, each=h_each(2 * l))
                pair_chunk(n + 1, h_rhs, blocks=((0, P),), width=P)
                n += 1
                pair_chunk(n + 1, h_rhs)
                pair_chunk(n + 2, h_rhs)
                pair_chunk(n + 3, h_rhs, blocks=((0, HD + NH),))

                pe.wait_ge(pair_evac, n + 3 - ADA_CHUNKS + 1)
                for t in range(3):
                    bank = (lg[:, 0:512], lg[:, 512:1024], px)[t]
                    for dst, src, k in ((0, kT, P), (P, ikT, P), (2 * P, viwT, HD + NH)):
                        ins = nc.tensor.transpose(bank[:, dst:dst + k], src[0:k, t * P:(t + 1) * P], ident[0:k, 0:k])
                    ins.then_inc(kv_tr, 1)

                def score_head(h):
                    s = slice(HD * (h % 2), HD * (h % 2) + HD)
                    if h == 0:
                        pe.wait_ge(kv_copied, 3 * (l + 1))
                    pe.wait_ge(rel_ready, 8 * l + h)
                    q = iqT[s, h // 2, :]
                    nc.tensor.matmul(px[:, 0:P], q[:, 0:P], ikT[s, 0:P], start=True, stop=True)
                    nc.tensor.matmul(py[:, 0:TP], q[:, P:TP], ikT[s, 0:TP], start=True, stop=True)
                    qs = q[:, TP:TP + 2 * TS]
                    nc.tensor.matmul(lg[:, 0:PAST], qs, ikTs[s, l, 0:PAST], start=True, stop=True)
                    nc.tensor.matmul(lg[:, PAST:NKS], qs, ikTs[s, l, PAST:NKS], start=True,
                                     stop=True).then_inc(sc_done, 1)

                order = [first["qkv", l] + 5, first["qkv", l] + 6] + [first["glu", l] + j for j in range(4)] \
                    + [first["cxs", l] + j for j in range(4)]
                for h, n in enumerate(order):
                    if h < NH:
                        score_head(h)
                    pair_chunk(n, h_rhs)
                for j in range(2):
                    pair_chunk(first["bgate", l] + j, h_rhs)

                pe.wait_ge(u_ready, 8 * (l + 1))
                pe.wait_ge(rel_ready, 8 * (l + 1))
                for s, (buf, c0, w) in enumerate(((u_conf, UC_P + TP - CH, CH), (u_conf, UC_S + TS - CH, CH),
                                                  (u_short, US_P + TP - SH, SH), (u_short, US_S + TS - SH, SH))):
                    bank = (lg[:, 0:512], lg[:, 512:1024], px, py)[s]
                    for j in range(BC):
                        ins = nc.tensor.transpose(bank[0:w, j * P:(j + 1) * P], buf[:, j, c0:c0 + w], ident[:])
                    ins.then_inc(st_tr, 1)

                def logits(u):
                    g = NUNITS * l + u
                    pe.wait_ge(lm_done, g) if g else None
                    if u < 8:
                        t, p, keys = u // 4, u % 4, P * (u // 4 + 1)
                        for h in range(2):
                            s = slice(HD * h, HD * h + HD)
                            ins = nc.tensor.matmul(lg[:, h * 512:h * 512 + keys], qT[s, p, t * P:(t + 1) * P],
                                                   kT[s, 0:keys], start=True, stop=True)
                    else:
                        for h in range(2):
                            s = slice(HD * h, HD * h + HD)
                            for a, b in ((0, PAST), (PAST, NKS)):
                                ins = nc.tensor.matmul(lg[s, a:b], qT[s, u - 8, TP:T], kTs[s, l, a:b],
                                                       start=True, stop=True)
                    ins.then_inc(lg_done, 1)

                def transposes(u):
                    g = NUNITS * l + u
                    pe.wait_ge(prob_ready, g + 1)
                    if g:
                        pe.wait_ge(pt_copied, g)
                    if u >= 8:
                        pe.wait_ge(attn_copied, g)
                    n_full = 2 * (u // 4 + 1) if u < 8 else 4
                    for i in range(n_full):
                        ins = nc.tensor.transpose(px[:, i * P:(i + 1) * P], prob[:, i * P:(i + 1) * P], ident[:])
                    if u >= 8:
                        ins = nc.tensor.transpose(py[0:TS, 3 * P:4 * P], prob[:, PAST:NKS], ident[:])
                    ins.then_inc(pt_done, 1)

                def values(u):
                    g = NUNITS * l + u
                    pe.wait_ge(pt_copied, g + 1)
                    if g:
                        pe.wait_ge(attn_copied, g)
                    for h in range(2):
                        s = slice(HD * h, HD * h + HD)
                        if u < 8:
                            nk = u // 4 + 1
                            ins = group(py[s, 0:P], [(kvtok[:, kc, 2 * P:2 * P + HD],
                                                      probT[:, u % 2, (h * nk + kc) * P:(h * nk + kc + 1) * P])
                                                     for kc in range(nk)])
                        else:
                            c = HD * h
                            prs = [(cv[:, l, kc, :], probT[:, u % 2, kc * P + c:kc * P + c + TS]) for kc in range(4)]
                            prs.append((kvtok[0:TS, 2, 2 * P:2 * P + HD], probT[0:TS, u % 2, 4 * P + c:4 * P + c + TS]))
                            ins = group(py[s, 0:TS], prs)
                    ins.then_inc(av_done, 1)

                pe.wait_ge(st_copied, 4 * (l + 1))

                def unit_tick(t):
                    if 0 <= t - 2 < NUNITS:
                        values(t - 2)
                    if 0 <= t < NUNITS:
                        logits(t)
                    if 0 <= t - 1 < NUNITS:
                        transposes(t - 1)

                for j in range(12):
                    unit_tick(j - 2)
                    pair_chunk(first["gates", l] + j, h_rhs)
                for j in range(4):
                    unit_tick(10 + j)
                    if j == 0:
                        pe.wait_ge(short_ready, l + 1)
                    pair_chunk(first["short", l] + j, lambda i: shortT[:, i, :], BC)

                pe.wait_ge(attn_copied, NUNITS * (l + 1))
                for j in range(4):
                    if j == 1:
                        pe.wait_ge(conv_ready, l + 1)
                        group(px[:, 0:TP], [(ones[:], conv[:, c, 0:TP]) for c in range(BC)])
                        group(px[:, TP:T], [(ones[:], conv[:, c, UC_S - CH:UC_S - CH + TS])
                                            for c in range(BC)]).then_inc(ln_sum, 1)
                    if j == 3:
                        pe.wait_ge(ln_sq, l + 1)
                        group(py[:, 0:T], [(ones[:], hT[:, BC + c, :]) for c in range(BC)]).then_inc(ln_ss, 1)
                    pair_chunk(first["attn", l] + j, lambda i: attnT[:, i, :], BC)
                pe.wait_ge(conf_ready, l + 1)
                for j in range(4):
                    pair_chunk(first["conf", l] + j, lambda i: confT[:, i, :], BC)
                for j in range(4):
                    pair_chunk(first["out", l] + j, lambda i: merged[:, i, :],
                               each=(lambda i: pe.wait_ge(merged_ready, 4 * l + i // 2 + 1)) if j == 0 else None)

                norm_sums(2 * l + 1)
                if l % 2 == 0:
                    def ffn_in(n, it=None):
                        pair_chunk(n, h_rhs, it=it)

                    def ffn_out(n, it=None):
                        pair_chunk(n, lambda i: hid[:, i, :], FC, ((0, P),), it, width=P)

                    for c in range(DC):
                        pe.wait_ge(h_ready, DC * (2 * l + 1) + c + 1)
                    n0 = first["ffn_in", l]
                    with pe.Fori(0, FC // SLOTS) as it:
                        for k in range(SLOTS):
                            ffn_in(n0 + k, it)
                    for k in range(FC - FC % SLOTS, FC):
                        ffn_in(n0 + k)
                    pe.wait_ge(hid_ready, FC)
                    with pe.Fori(0, DC // SLOTS) as it:
                        for k in range(SLOTS):
                            ffn_out(first["ffn_out", l] + k, it)
                else:
                    for c in range(DC):
                        pe.wait_ge(h_ready, DC * (2 * l + 1) + c + 1)
                    pe.wait_ge(router_loaded, 32)
                    for t in range(3):
                        m = P if t < 2 else TS
                        ts = slice(t * P, t * P + m)
                        ins = group(px[0:m, t * NE:(t + 1) * NE],
                                    [(hT[:, c, ts], wr[:, c, :]) for c in range(DC)] + [(ones[0:1, 0:m], br[0:1, :])])
                    ins.then_inc(rt_done, 1)
                    pe.wait_ge(comb_ready, 1)
                    for e in range(NE):
                        if e >= 2:
                            pe.wait_ge(cb_copied, e - 1)
                        o = (e % 2) * 512
                        for t in range(3):
                            m = P if t < 2 else TS
                            ins = nc.tensor.matmul(lg[:, o + t * P:o + t * P + m],
                                                   comb[0:m, t, e:e + 1].broadcast_to([m, P]), ident[0:m, 0:m],
                                                   start=True, stop=True)
                        ins.then_inc(cb_done, 1)
                    n0 = first["moe", l]
                    with pe.Fori(0, NE) as e:
                        for k in range(15):
                            n = n0 + k
                            fills = 4 if n % SLOTS != (n0 + 15) % SLOTS else 3
                            pe.wait_ge(w_full[n % SLOTS], e * (32 * fills) + 32 * (n // SLOTS + 1))
                            pe.wait_ge(pair_evac, e * 15 + (n - ADA_CHUNKS - (k > 0)))
                            kk, src = (DC, hT) if k < EC else (EC, hid)
                            v = slot_view(n % SLOTS, kk, 2 * P)
                            for b in range(2):
                                for i in range(kk):
                                    if k == EC and b == 0:
                                        pe.wait_ge(hid_ready, e * EC + (FC + i + 1))
                                    ins = nc.tensor.matmul(mmp[:, 2 * (k % 2) + b, 0:T], v[:, i, b * P:(b + 1) * P],
                                                           src[:, i, :], start=(i == 0), stop=(i == kk - 1))
                            ins.then_inc(chunk_done, 1 if k < 14 else 2)

            norm_sums(4)
            pe.wait_ge(h_ready, DC * 5)
            for b in range(6):
                t, g = b // 2, b % 2
                m = P if t < 2 else TS
                if b >= 4:
                    pe.wait_ge(y_copied, b - 3)
                for j in range(4):
                    ins = nc.tensor.transpose(mmp[0:m, b % 4, j * P:(j + 1) * P], hT[:, 4 * g + j, t * P:t * P + m],
                                              ident[:])
                ins.then_inc(y_tr, 1)

        @block.scalar
        def _(act):
            copy = nc.scalar.copy

            for l in range(DEPTH):
                v = vrows[:, l, 0, :]
                for row, ap, k in ((R_BADA, b_ada[l], 48), (R_GMIX, g_norm_mix[l], 8), (R_GFFN, g_norm_ffn[l], 8),
                                   (R_BDW, b_dw_conf[l], 4), (R_LNG, ln_conf_g[l], 4), (R_LNB, ln_conf_b[l], 4),
                                   (R_GFIN, g_final, 8), (R_C, c_prompt[0], 8), (R_C + 8, c_sample[0], 8)):
                    act.dma_start(v[row:row + k, :], ap.rearrange("(c p) -> c p", p=P)).then_inc(rows_loaded, 16)
                for w in range(SW):
                    act.dma_start(v[R_WSH + 4 * w:R_WSH + 4 * w + 4, :],
                                  w_dw_short[l, w].rearrange("(c p) -> c p", p=P)).then_inc(rows_loaded, 16)
                act.dma_start(vrows[0:CW * BC, l, 1, :],
                              w_dw_conf[l].rearrange("w (c p) -> (w c) p", p=P)).then_inc(rows_loaded, 16)
            act.dma_start(x_tok[:, 0:2, :], x_prompt[0].rearrange("(t p) d -> p t d", p=P)).then_inc(x_loaded, 16)
            act.dma_start(x_tok[0:TS, 2, :], x_sample[0]).then_inc(x_loaded, 16)
            for l in range(DEPTH):
                for m, cache in enumerate((cache_k, cache_idx_k)):
                    src = cache[l, 0].rearrange("(k p) d -> p k d", p=P)
                    for r in range(2):
                        act.dma_start(craw[:, l, m, :, r * HD:(r + 1) * HD], src).then_inc(caches_loaded, 16)
                act.dma_start(hraw[0:CH, l, 0, :], state_conv_conformer[l, 0]).then_inc(caches_loaded, 16)
                act.dma_start(hraw[0:SH, l, 1, :], state_conv_short[l, 0]).then_inc(caches_loaded, 16)
                act.dma_start(cv[:, l, :, :], cache_v[l, 0].rearrange("(k p) d -> p k d", p=P)).then_inc(caches_loaded, 16)
            act.dma_start(wr[:], w_router[0].rearrange("(c p) e -> p c e", p=P)).then_inc(router_loaded, 16)
            act.dma_start(br[:], b_router[0:1, :]).then_inc(router_loaded, 16)

            act.wait_ge(pro_copied, 1)
            for s in range(2):
                ins = nc.scalar.activation(cT[:, :, s], vec[:, 0, R_C + 8 * s:R_C + 8 * s + 8], ACT.Silu)
            ins.then_inc(c_ready, 1)

            def norm(k, gain_of, shift_of):
                act.wait_ge(x_ready, k + 1)
                nc.scalar.activation(sq[:], xT[:], ACT.Square).then_inc(sq_ready, 1)
                act.wait_ge(ms_ready, k + 1)
                nc.scalar.activation(std[:], var[:], ACT.Sqrt).then_inc(std_ready, 1)
                for c in range(DC):
                    act.wait_ge(xn_ready, DC * k + c + 1)
                    for s, ts in enumerate((slice(0, TP), slice(TP, T))):
                        b = shift_of(c, s)
                        ins = nc.scalar.activation(hT[:, c, ts], hT[:, c, ts], ACT.Identity, scale=gain_of(c, s),
                                                   bias=0.0 if b is None else b)
                    ins.then_inc(h_ready, 1)

            def chunk_wait(n, it=None, per=SLOTS):
                act.wait_ge(chunk_done, n + 1 if it is None else it * per + (n + 1))

            def pair(n, b, m=P):
                return mmp[0:m, 2 * (n % 2) + b, 0:T]

            def to_tmp(n, t, f0, f1, it=None):
                chunk_wait(n, it)
                if it is not None:
                    act.wait_ge(tmp_free, it * SLOTS + (t - 1))
                elif t >= 2:
                    act.wait_ge(tmp_free, t - 1)
                ins = nc.scalar.activation(tmp[:, t % 2, 0, :], pair(n, 0), f0)
                if f1 is not None:
                    ins = nc.scalar.activation(tmp[:, t % 2, 1, :], pair(n, 1), f1)
                ins.then_inc(tmp_ready, 1)
                act.wait_ge(tmp_ready, (t + 1) if it is None else it * SLOTS + (t + 1))
                act.sem_inc(pair_evac, 1)

            for l in range(DEPTH):
                def gain_of(which):
                    return lambda c, s: gain[:, l, which, c, s:s + 1]

                def shift_of(which):
                    return lambda c, s: mods[:, l, 24 * which + c, s:s + 1]

                if l == 0:
                    act.wait_ge(mods_ready, 1)
                norm(2 * l, gain_of(0), shift_of(0))

                n = first["qkv", l]
                chunk_wait(n)
                copy(kT[:, 0:T], pair(n, 0))
                copy(kT[:, T:TW], pair(n, 0)[:, TP:T])
                copy(kTs[:, l, PAST:NKS], pair(n, 0)[:, TP:T]).then_inc(pair_evac, 1)
                n += 1
                chunk_wait(n)
                copy(ikT[:, 0:T], pair(n, 0))
                copy(ikT[:, T:TW], pair(n, 0)[:, TP:T])
                copy(ikTs[:, l, PAST:NKS], pair(n, 0)[:, TP:T]).then_inc(pair_evac, 1)
                for j in range(2):
                    chunk_wait(n + 1 + j)
                    for b in range(2):
                        copy(iqT[:, 2 * j + b, 0:T], pair(n + 1 + j, b))
                        ins = copy(iqT[:, 2 * j + b, T:TW], pair(n + 1 + j, b)[:, TP:T])
                    ins.then_inc(pair_evac, 1)
                chunk_wait(n + 3)
                copy(viwT[0:HD + NH, 0:T], pair(n + 3, 0, HD + NH))
                copy(viwT[0:HD + NH, T:TW], pair(n + 3, 0, HD + NH)[:, TP:T]).then_inc(pair_evac, 1)

                if l:
                    act.wait_ge(stored, 16 * 10 * l)
                for t in range(3):
                    act.wait_ge(kv_tr, 3 * l + t + 1)
                    bank = (lg[:, 0:512], lg[:, 512:1024], px)[t]
                    copy(kvtok[:, t, :], bank[:, 0:328]).then_inc(kv_copied, 1)
                act.wait_ge(kv_copied, 3 * (l + 1))
                for dst_p, dst_s, c0 in ((pk, sk, 0), (pik, sik, P), (pv, sv, 2 * P)):
                    act.dma_start(dst_p[l, 0].rearrange("(t p) d -> p t d", p=P),
                                  kvtok[:, 0:2, c0:c0 + HD]).then_inc(stored, 16)
                    act.dma_start(dst_s[l, 0], kvtok[0:TS, 2, c0:c0 + HD]).then_inc(stored, 16)

                def relu_head(h):
                    g = 8 * l + h
                    act.wait_ge(sc_done, g + 1)
                    if g >= 2:
                        act.wait_ge(rel_used, g - 1)
                    nc.scalar.activation(rel[:, h % 2, 0:P], px[:, 0:P], ACT.Relu, scale=HD ** -0.5)
                    nc.scalar.activation(rel[:, h % 2, P:P + TP], py[:, 0:TP], ACT.Relu, scale=HD ** -0.5)
                    nc.scalar.activation(rel[:, h % 2, P + TP:960], lg[:, 0:NKS], ACT.Relu,
                                         scale=HD ** -0.5).then_inc(rel_ready, 1)

                for h in range(10):
                    if h < NH:
                        relu_head(h)
                    if h < 2:
                        n = first["qkv", l] + 5 + h
                        chunk_wait(n)
                        copy(qT[:, 2 * h, :], pair(n, 0))
                        copy(qT[:, 2 * h + 1, :], pair(n, 1)).then_inc(pair_evac, 1)
                    elif h < 6:
                        to_tmp(first["glu", l] + h - 2, tmp_before["glu", l] + h - 2, ACT.Copy, ACT.Sigmoid)
                    else:
                        to_tmp(first["cxs", l] + h - 6, tmp_before["cxs", l] + h - 6, ACT.Copy, ACT.Copy)
                for j in range(2):
                    n = first["bgate", l] + j
                    chunk_wait(n)
                    copy(bgate[:, 2 * j, :], pair(n, 0))
                    copy(bgate[:, 2 * j + 1, :], pair(n, 1)).then_inc(pair_evac, 1)

                for s, (w, dst) in enumerate(((CH, pconf), (CH, sconf), (SH, pshort), (SH, sshort))):
                    act.wait_ge(st_tr, 4 * l + s + 1)
                    bank = (lg[:, 0:512], lg[:, 512:1024], px, py)[s]
                    copy(st_out[0:w, s, :], bank[0:w, :]).then_inc(st_copied, 1)
                    act.wait_ge(st_copied, 4 * l + s + 1)
                    act.dma_start(dst[l, 0], st_out[0:w, s, :]).then_inc(stored, 16)

                def attn_copy(u):
                    act.wait_ge(av_done, NUNITS * l + u + 1)
                    if u < 8:
                        dst, src = attnT[:, u % 4, (u // 4) * P:(u // 4 + 1) * P], py[:, 0:P]
                    else:
                        dst, src = attnT[:, u - 8, TP:T], py[:, 0:TS]
                    copy(dst, src).then_inc(attn_copied, 1)

                def pt_copy(u):
                    g = NUNITS * l + u
                    act.wait_ge(pt_done, g + 1)
                    if g >= 2:
                        act.wait_ge(av_done, g - 1)
                    w = 2 * P * (u // 4 + 1) if u < 8 else 4 * P
                    ins = copy(probT[:, u % 2, 0:w], px[:, 0:w])
                    if u >= 8:
                        ins = copy(probT[0:TS, u % 2, 4 * P:5 * P], py[0:TS, 3 * P:4 * P])
                    ins.then_inc(pt_copied, 1)

                def exp(u):
                    g = NUNITS * l + u
                    act.wait_ge(lm_done, g + 1)
                    if g:
                        act.wait_ge(pt_done, g)
                    if u < 8:
                        keys = P * (u // 4 + 1)
                        for h in range(2):
                            s = slice(h * keys, (h + 1) * keys)
                            ins = nc.scalar.activation(prob[:, s], lm[:, s], ACT.Exp, bias=nmax[:, h:h + 1],
                                                       accum_out=psums[:, h:h + 1])
                    else:
                        ins = nc.scalar.activation(prob[:, 0:NKS], lm[:, 0:NKS], ACT.Exp, bias=nmax[:, 0:1],
                                                   accum_out=psums[:, 0:1])
                    ins.then_inc(exp_done, 1)

                def unit_tick(t):
                    if 0 <= t - 2 < NUNITS:
                        attn_copy(t - 2)
                    if 0 <= t - 1 < NUNITS:
                        pt_copy(t - 1)
                    if 0 <= t < NUNITS:
                        exp(t)

                for j in range(12):
                    unit_tick(j - 2)
                    n = first["gates", l] + j
                    chunk_wait(n)
                    nc.scalar.activation(gates[:, 2 * j, :], pair(n, 0), ACT.Sigmoid)
                    nc.scalar.activation(gates[:, 2 * j + 1, :], pair(n, 1), ACT.Sigmoid).then_inc(pair_evac, 1)
                for j in range(4):
                    unit_tick(10 + j)
                    to_tmp(first["short", l] + j, tmp_before["short", l] + j, ACT.Copy, ACT.Copy)

                for j in range(4):
                    to_tmp(first["attn", l] + j, tmp_before["attn", l] + j, ACT.Copy, ACT.Copy)
                    if j == 1:
                        act.wait_ge(xc_ready, l + 1)
                        nc.scalar.activation(hT[:, BC:2 * BC, :], hT[:, 0:BC, :], ACT.Square).then_inc(ln_sq, 1)
                act.wait_ge(ln_ms, l + 1)
                nc.scalar.activation(std[:], var[:], ACT.Sqrt).then_inc(ln_std, 1)
                act.wait_ge(ln_n, l + 1)
                for c in range(BC):
                    ins = nc.scalar.activation(confT[:, c, :], hT[:, c, :], ACT.Silu,
                                               scale=vec[:, l, R_LNG + c:R_LNG + c + 1],
                                               bias=vec[:, l, R_LNB + c:R_LNB + c + 1])
                ins.then_inc(conf_ready, 1)
                for stage in ("conf", "out"):
                    for j in range(4):
                        to_tmp(first[stage, l] + j, tmp_before[stage, l] + j, ACT.Copy, ACT.Copy)

                norm(2 * l + 1, gain_of(1), shift_of(1))
                if l % 2 == 0:
                    n0, t0 = first["ffn_in", l], tmp_before["ffn_in", l]
                    with act.Fori(0, FC // SLOTS) as it:
                        for k in range(SLOTS):
                            to_tmp(n0 + k, t0 + k, ACT.Silu, ACT.Copy, it)
                    for k in range(FC - FC % SLOTS, FC):
                        to_tmp(n0 + k, t0 + k, ACT.Silu, ACT.Copy)
                    n0, t0 = first["ffn_out", l], tmp_before["ffn_out", l]
                    with act.Fori(0, DC // SLOTS) as it:
                        for k in range(SLOTS):
                            to_tmp(n0 + k, t0 + k, ACT.Copy, None, it)
                else:
                    act.wait_ge(rt_d, 1)
                    nc.scalar.activation(rsc[:, 3:6], rsc[:, 0:3], ACT.Exp).then_inc(rt_e, 1)
                    act.wait_ge(stored, 16 * 10 * DEPTH)
                    for e in range(NE):
                        act.wait_ge(cb_done, e + 1)
                        copy(comb_bc[:, e, :], lg[:, (e % 2) * 512:(e % 2) * 512 + T]).then_inc(cb_copied, 1)
                    n0, t0 = first["moe", l], tmp_before["moe", l]
                    with act.Fori(0, NE) as e:
                        for k in range(15):
                            t = t0 + k
                            act.wait_ge(chunk_done, e * 16 + (n0 + k + 1))
                            act.wait_ge(tmp_free, e * 15 + (t - (k > 0)))
                            nc.scalar.activation(tmp[:, k % 2, 0, :], mmp[:, 2 * (k % 2), 0:T],
                                                 ACT.Silu if k < EC else ACT.Copy)
                            nc.scalar.activation(tmp[:, k % 2, 1, :], mmp[:, 2 * (k % 2) + 1, 0:T],
                                                 ACT.Copy).then_inc(tmp_ready, 1)
                            act.wait_ge(tmp_ready, e * 15 + (t + 1))
                            act.sem_inc(pair_evac, 1)

            norm(4, lambda c, s: vec[:, 0, R_GFIN + c:R_GFIN + c + 1], lambda c, s: None)
            for t in range(3):
                act.wait_ge(y_copied, 2 * (t + 1))
                if t < 2:
                    act.dma_start(y_prompt[0, t * P:(t + 1) * P, :], x_tok[:, t, :]).then_inc(y_stored, 16)
                else:
                    act.dma_start(y_sample[0], x_tok[0:TS, t, :]).then_inc(y_stored, 16)
            act.wait_ge(y_stored, 48)
            act.wait_ge(stored, 16 * 10 * DEPTH)

        @block.vector
        def _(dve):
            V = nc.vector
            steps = [0]

            def link(ins):
                steps[0] += 1
                ins.then_inc(dve_step, 1)
                dve.wait_ge(dve_step, steps[0])

            b = 0

            def pro(dst, src):
                nonlocal b
                dve.wait_ge(pro_tr, b + 1)
                if not isinstance(dst, list):
                    dst, src = [dst], [src]
                for i, (d, s) in enumerate(zip(dst, src)):
                    ins = V.tensor_copy(d, s(mmp[:, b % 4, :]))
                ins.then_inc(pro_copied, 1)
                b += 1

            for l in range(DEPTH):
                dve.wait_ge(pro_tr, b + 1)
                link(V.tensor_copy(vec[:, l, :], mmp[:, b % 4, 0:NROWS]))
                V.tensor_copy(dwc[:, l, :], mmp[:, b % 4, P:P + CW * BC]).then_inc(pro_copied, 1)
                b += 1
            for t in range(3):
                m = P if t < 2 else TS
                for g in range(2):
                    pro(xT[:, 4 * g:4 * g + 4, t * P:t * P + m],
                        lambda s: s.rearrange("p (j t) -> p j t", j=4)[:, :, 0:m])
            for l in range(DEPTH):
                for dst in (kTs, ikTs):
                    pro(dst[:, l, 0:PAST], lambda s: s)
                pro(hist[:, l, :, :], lambda s: s[:, 0:P].rearrange("p (j t) -> p j t", j=4))

            for l in range(DEPTH):
                dve.wait_ge(chunk_done, first["ada", l] + 24)
                bank = (px, py)[l]
                bias = vec[:, l, R_BADA:R_BADA + 48].unsqueeze(2).broadcast_to([P, 48, 2])
                link(V.tensor_tensor(mods[:, l, :, :], bank[:, 0:96].rearrange("p (j s) -> p j s", s=2), bias, ALU.add))
                for w, r in ((0, R_GMIX), (1, R_GFFN)):
                    link(V.tensor_scalar(gain[:, l, w, :, :], mods[:, l, 24 * w + 8:24 * w + 16, :], 1.0, None, ALU.add))
                    link(V.tensor_tensor(gain[:, l, w, :, :], gain[:, l, w, :, :],
                                         vec[:, l, r:r + 8].unsqueeze(2).broadcast_to([P, DC, 2]), ALU.mult))
            dve.wait_ge(pro_copied, 14)
            dve.sem_inc(mods_ready, 1)
            dve.sem_inc(x_ready, 1)

            def norm(k):
                dve.wait_ge(sum_ready, k + 1)
                V.tensor_scalar(var[:], py[:, 0:T], 1.0 / D, EPS, ALU.mult, ALU.add).then_inc(ms_ready, 1)
                dve.wait_ge(std_ready, k + 1)
                link(V.reciprocal(rstd[:], std[:]))
                for c in range(DC):
                    V.tensor_tensor(hT[:, c, :], xT[:, c, :], rstd[:], ALU.mult).then_inc(xn_ready, 1)

            def bcast(ap, n, w):
                return ap.unsqueeze(1).broadcast_to([P, n, w])

            score_areas = ((0, P, TOPK_P), (P, P + TP, TOPK_P), (P + TP, 960, TOPK_S))

            for l in range(DEPTH):
                norm(2 * l)

                dve.wait_ge(kv_copied, 3 * (l + 1))
                link(V.tensor_scalar(iws[:], kvtok[:, :, 2 * P + HD:2 * P + HD + NH], NH ** -0.5, None, ALU.mult))
                for h in range(NH):
                    dve.wait_ge(rel_ready, 8 * l + h + 1)
                    for t, (a, z, _) in enumerate(score_areas):
                        w = iws[:, t, h:h + 1]
                        if h == 0:
                            ins = V.tensor_scalar(score[:, a:z], rel[:, 0, a:z], w, None, ALU.mult)
                        else:
                            ins = V.scalar_tensor_tensor(score[:, a:z], rel[:, h % 2, a:z], w, score[:, a:z],
                                                         ALU.mult, ALU.add)
                    ins.then_inc(rel_used, 1)
                    dve.wait_ge(rel_used, 8 * l + h + 1)

                link(V.memset(score[0:CHUNK, CHUNK:P], INADMISSIBLE))
                link(V.memset(score[0:CHUNK, P + TP - CHUNK:P + TP], INADMISSIBLE))

                for a, z, k in score_areas:
                    for r in range(k // 8):
                        src = score if r == 0 else work
                        link(V.max(out=top8[:], in_=src[:, a:z]))
                        link(V.match_replace(out=work[:, a:z], in_to_replace=top8[:], in_values=src[:, a:z],
                                             imm_value=TAKEN))
                    link(V.tensor_scalar(score[:, a:z], work[:, a:z], TAKEN, NEG_MASK, ALU.is_gt, ALU.mult))
                mask = score

                dve.wait_ge(u_ready, 8 * (l + 1))
                dve.wait_ge(hist_ready, l + 1)
                w_sh = USW - SH
                for w in range(SW):
                    for c in range(BC):
                        tap = vec[:, l, R_WSH + 4 * w + c:R_WSH + 4 * w + c + 1]
                        src = u_short[:, c, w:w + w_sh]
                        if w == 0:
                            ins = V.tensor_scalar(sconv[:, c, :], src, tap, None, ALU.mult)
                        else:
                            ins = V.scalar_tensor_tensor(sconv[:, c, :], src, tap, sconv[:, c, :], ALU.mult, ALU.add)
                    link(ins)
                dve.wait_ge(pair_evac, first["bgate", l] + 2 - ADA_CHUNKS)
                dve.wait_ge(st_tr, 4 * (l + 1))
                for src, ts in segs(sconv, 0, US_S - SH):
                    link(V.tensor_tensor(shortT[:, :, ts], src, bgate[:, :, ts], ALU.mult))
                dve.sem_inc(short_ready, 1)

                taps = [(w, c) for w in range(CW) for c in range(BC)]
                w_cv = UCW - CH

                def conv_taps(count):
                    for w, c in taps[:count]:
                        tap = dwc[:, l, w * BC + c:w * BC + c + 1]
                        src = u_conf[:, c, w:w + w_cv]
                        if w == 0:
                            ins = V.tensor_scalar(conv[:, c, :], src, tap, vec[:, l, R_BDW + c:R_BDW + c + 1],
                                                  ALU.mult, ALU.add)
                        else:
                            ins = V.scalar_tensor_tensor(conv[:, c, :], src, tap, conv[:, c, :], ALU.mult, ALU.add)
                        if c == BC - 1:
                            link(ins)
                    del taps[:count]

                for u in range(NUNITS):
                    g = NUNITS * l + u
                    dve.wait_ge(lg_done, g + 1)
                    if u < 8:
                        keys = P * (u // 4 + 1)
                        a = 0 if u < 4 else P
                        v3 = lm[:, 0:2 * keys].rearrange("p (h k) -> p h k", h=2)
                        link(V.scalar_tensor_tensor(v3, lg[:, :].rearrange("p (h k) -> p h k", h=2)[:, :, 0:keys],
                                                    HD ** -0.5, bcast(mask[:, a:a + keys], 2, keys),
                                                    ALU.mult, ALU.add))
                        V.tensor_reduce(nmax[:, 0:2], v3, AX, ALU.max, negate=True).then_inc(lm_done, 1)
                    else:
                        link(V.scalar_tensor_tensor(lm[:], lg[:, 0:NKS], HD ** -0.5, mask[:, P + TP:960],
                                                    ALU.mult, ALU.add))
                        V.tensor_reduce(nmax[:, 0:1], lm[:], AX, ALU.max, negate=True).then_inc(lm_done, 1)
                    conv_taps(8)
                    dve.wait_ge(exp_done, g + 1)
                    if u < 8:
                        link(V.reciprocal(prec[:], psums[:]))
                        v3 = prob[:, 0:2 * keys].rearrange("p (h k) -> p h k", h=2)
                        V.tensor_tensor(v3, v3, prec[:].unsqueeze(2).broadcast_to([P, 2, keys]),
                                        ALU.mult).then_inc(prob_ready, 1)
                    else:
                        link(V.reciprocal(prec[:, 0:1], psums[:, 0:1]))
                        V.tensor_scalar(prob[:], prob[:], prec[:, 0:1], None, ALU.mult).then_inc(prob_ready, 1)
                conv_taps(len(taps))
                dve.sem_inc(conv_ready, 1)

                def merge(stage, j, gate0, is_first):
                    t = tmp_before[stage, l] + j
                    dve.wait_ge(tmp_ready, t + 1)
                    both = tmp[:, t % 2, :, :]
                    g_ap = gates[:, gate0 + 2 * j:gate0 + 2 * j + 2, :]
                    dst = merged[:, 2 * j:2 * j + 2, :]
                    if is_first:
                        V.tensor_tensor(dst, both, g_ap, ALU.mult).then_inc(tmp_free, 1)
                        dve.wait_ge(tmp_free, t + 1)
                    else:
                        link(V.tensor_tensor(both, both, g_ap, ALU.mult))
                        V.tensor_tensor(dst, dst, both, ALU.add).then_inc(tmp_free, 1)
                        dve.wait_ge(tmp_free, t + 1)

                dve.wait_ge(tmp_free, tmp_before["short", l])
                for j in range(4):
                    merge("short", j, 2 * DC, True)
                for j in range(4):
                    merge("attn", j, 0, False)
                    if j == 1:
                        dve.wait_ge(ln_sum, l + 1)
                        link(V.tensor_scalar(mean[:], px[:, 0:T], 1.0 / DB, None, ALU.mult))
                        for src, ts in segs(conv, 0, UC_S - CH):
                            ins = V.tensor_tensor(hT[:, 0:BC, ts], src, bcast(mean[:, ts], BC, ts.stop - ts.start),
                                                  ALU.subtract)
                            link(ins)
                        dve.sem_inc(xc_ready, 1)
                dve.wait_ge(ln_ss, l + 1)
                V.tensor_scalar(var[:], py[:, 0:T], 1.0 / DB, EPS, ALU.mult, ALU.add).then_inc(ln_ms, 1)
                dve.wait_ge(ln_std, l + 1)
                link(V.reciprocal(rstd[:], std[:]))
                V.tensor_tensor(hT[:, 0:BC, :], hT[:, 0:BC, :], bcast(rstd[:], BC, T), ALU.mult).then_inc(ln_n, 1)
                for j in range(4):
                    merge("conf", j, DC, False)
                    dve.sem_inc(merged_ready, 1)

                def add_to_x(j, src, which):
                    for s, ts in enumerate((slice(0, TP), slice(TP, T))):
                        ins = V.scalar_tensor_tensor(xT[:, j, ts], src[:, ts], mods[:, l, 24 * which + 16 + j, s:s + 1],
                                                     xT[:, j, ts], ALU.mult, ALU.add)
                    return ins

                for j in range(4):
                    t = tmp_before["out", l] + j
                    dve.wait_ge(tmp_ready, t + 1)
                    add_to_x(2 * j, tmp[:, t % 2, 0, :], 0)
                    add_to_x(2 * j + 1, tmp[:, t % 2, 1, :], 0).then_inc(tmp_free, 1)
                dve.wait_ge(tmp_free, tmp_before["out", l] + 4)
                dve.sem_inc(x_ready, 1)

                norm(2 * l + 1)
                if l % 2 == 0:
                    t0 = tmp_before["ffn_in", l]

                    def gate_up(t, f, wait_to):
                        dve.wait_ge(tmp_ready, wait_to)
                        V.tensor_tensor(f, tmp[:, t % 2, 0, :], tmp[:, t % 2, 1, :], ALU.mult).then_inc(hid_ready, 1)

                    with dve.Fori(0, FC // SLOTS) as it:
                        for k in range(SLOTS):
                            f = hid[:, bass.ds(it * SLOTS + k, 1), :].rearrange("p a t -> p (a t)")
                            gate_up(t0 + k, f, it * SLOTS + (t0 + k + 1))
                            dve.wait_ge(hid_ready, it * SLOTS + (k + 1))
                            dve.sem_inc(tmp_free, 1)
                    for k in range(FC - FC % SLOTS, FC):
                        gate_up(t0 + k, hid[:, k, :], t0 + k + 1)
                        dve.wait_ge(hid_ready, k + 1)
                        dve.sem_inc(tmp_free, 1)
                    t0 = tmp_before["ffn_out", l]
                    for k in range(DC):
                        dve.wait_ge(tmp_ready, t0 + k + 1)
                        add_to_x(k, tmp[:, (t0 + k) % 2, 0, :], 1).then_inc(tmp_free, 1)
                    dve.wait_ge(tmp_free, t0 + DC)
                else:
                    dve.wait_ge(rt_done, 1)
                    link(V.memset(comb[:], 0.0))
                    link(V.memset(rsc[:], 0.0))
                    tops = []
                    for t in range(3):
                        m = P if t < 2 else TS
                        link(V.tensor_copy(rl[0:m, t, :], px[0:m, t * NE:(t + 1) * NE]))
                        link(V.max(out=top8[0:m, :], in_=rl[0:m, t, :]))
                        link(V.max_index(out=idx_u[0:m, :], in_max=top8[0:m, :], in_values=rl[0:m, t, :]))
                        link(V.tensor_copy(idx_f[0:m, 2 * t:2 * t + 2], idx_u[0:m, 0:2]))
                        link(V.tensor_tensor(rsc[0:m, t:t + 1], top8[0:m, 1:2], top8[0:m, 0:1], ALU.subtract))
                    dve.sem_inc(rt_d, 1)
                    dve.wait_ge(rt_e, 1)
                    link(V.tensor_scalar(rsc[:, 0:3], rsc[:, 3:6], 1.0, None, ALU.add))
                    link(V.reciprocal(rsc[:, 0:3], rsc[:, 0:3]))
                    link(V.tensor_tensor(rsc[:, 3:6], rsc[:, 3:6], rsc[:, 0:3], ALU.mult))
                    for t in range(3):
                        m = P if t < 2 else TS
                        link(V.tensor_scalar(comb[0:m, t, :], iota_f[0:m, :], idx_f[0:m, 2 * t:2 * t + 1],
                                             rsc[0:m, t:t + 1], ALU.is_equal, ALU.mult))
                        link(V.tensor_scalar(comb2[0:m, :], iota_f[0:m, :], idx_f[0:m, 2 * t + 1:2 * t + 2],
                                             rsc[0:m, 3 + t:4 + t], ALU.is_equal, ALU.mult))
                        link(V.tensor_tensor(comb[0:m, t, :], comb[0:m, t, :], comb2[0:m, :], ALU.add))
                    dve.sem_inc(comb_ready, 1)
                    link(V.memset(acc[:], 0.0))
                    dve.wait_ge(cb_copied, NE)

                    t0 = tmp_before["moe", l]
                    with dve.Fori(0, NE) as e:
                        for k in range(EC):
                            dve.wait_ge(tmp_ready, e * 15 + (t0 + k + 1))
                            V.tensor_tensor(hid[:, k, :], tmp[:, k % 2, 0, :], tmp[:, k % 2, 1, :],
                                            ALU.mult).then_inc(hid_ready, 1)
                            dve.wait_ge(hid_ready, e * EC + (FC + k + 1))
                            dve.sem_inc(tmp_free, 1)
                        cb = comb_bc[:, bass.ds(e, 1), :].broadcast_to([P, 2, T])
                        for k in range(4):
                            dve.wait_ge(tmp_ready, e * 15 + (t0 + EC + k + 1))
                            both = tmp[:, (EC + k) % 2, :, :]
                            V.tensor_tensor(both, both, cb, ALU.mult).then_inc(dve_step, 1)
                            dve.wait_ge(dve_step, e * 4 + (steps[0] + k + 1))
                            dst = acc[:, 2 * k:2 * k + 2, :]
                            V.tensor_tensor(dst, dst, both, ALU.add).then_inc(tmp_free, 1)
                    steps[0] += 4 * NE
                    dve.wait_ge(tmp_free, t0 + 15 * NE)
                    for j in range(DC):
                        ins = add_to_x(j, acc[:, j, :], 1)
                    link(ins)
                dve.sem_inc(x_ready, 1)

            norm(4)
            for b in range(6):
                t, g = b // 2, b % 2
                m = P if t < 2 else TS
                dve.wait_ge(y_tr, b + 1)
                V.tensor_copy(x_tok[0:m, t, g * 512:(g + 1) * 512], mmp[0:m, b % 4, :]).then_inc(y_copied, 1)


_INS = ['x_prompt', 'x_sample', 'cache_k', 'cache_v', 'cache_idx_k', 'state_conv_conformer', 'state_conv_short',
        'c_prompt', 'c_sample', 'w_ada', 'b_ada', 'g_norm_mix', 'g_norm_ffn', 'w_in', 'w_dw_conf', 'b_dw_conf',
        'ln_conf_g', 'ln_conf_b', 'w_dw_short', 'w_branch', 'w_out', 'w_ffn_in', 'w_ffn_out', 'w_router', 'b_router',
        'w_exp_in', 'w_exp_out', 'g_final']
_OUTS = [(1, TP, D), (1, TS, D),
         (DEPTH, 1, TP, HD), (DEPTH, 1, TP, HD), (DEPTH, 1, TP, HD), (DEPTH, 1, CH, DB), (DEPTH, 1, SH, DB),
         (DEPTH, 1, TS, HD), (DEPTH, 1, TS, HD), (DEPTH, 1, TS, HD), (DEPTH, 1, CH, DB), (DEPTH, 1, SH, DB)]


def kernel(**inputs):
    import numpy as _np
    import concourse.bacc as _bacc
    from concourse import mybir as _mybir
    from concourse.bass_utils import run_bass_kernel_spmd as _run

    nc = _bacc.Bacc("TRN2", target_bir_lowering=False, num_devices=1)
    arrays, args = {}, []
    for name in _INS:
        a = _np.ascontiguousarray(inputs[name])
        arrays[f"in_{name}_dram"] = a
        args.append(nc.dram_tensor(f"in_{name}_dram", a.shape, _mybir.dt.from_np(a.dtype), kind="ExternalInput").ap())
    for i, shape in enumerate(_OUTS):
        args.append(nc.dram_tensor(f"out_{i}_dram", shape, _mybir.dt.float32, kind="ExternalOutput").ap())
    build(nc, *args)
    r = _run(nc, [arrays], core_ids=[0])
    return tuple(r.results[0][f"out_{i}_dram"] for i in range(len(_OUTS)))
```

```python
from contextlib import ExitStack

import numpy as np

import concourse.bass as bass
from concourse import mybir

F32 = mybir.dt.float32
F32R = mybir.dt.float32r
U32 = mybir.dt.uint32
I32 = mybir.dt.int32
ALU = mybir.AluOpType
ACT = mybir.ActivationFunctionType
AX = mybir.AxisListType.X

P = 128
D = 1024
DC = D // P
TP, TS = 256, 64
T = TP + TS
TW = T + TS
DEPTH = 2
PAST = 512
NKS = PAST + TS
CHUNK = 64
NH, HD = 8, 64
DA = NH * HD
TOPK_P = min(256, TP // 4)
TOPK_S = min(256, NKS // 4)
DB = 512
BC = DB // P
CW, SW = 31, 3
DFF, DFE, NE = 2816, 1408, 8
FC, EC = DFF // P, DFE // P
EPS = 1e-6

Q0 = 0
K0 = Q0 + DA
V0 = K0 + HD
IQ0 = V0 + HD
IK0 = IQ0 + DA
IW0 = IK0 + HD
GLU0 = IW0 + NH
SC0 = GLU0 + 2 * DB
GATE0 = SC0 + 3 * DB

NEG_MASK = -1e30
INADMISSIBLE = -1e38
TAKEN = float(np.float32(-3e38))

CH, SH = CW - 1, SW - 1
UCW = 2 * CH + T
USW = 2 * SH + T
UC_P, UC_S = CH, 2 * CH + TP
US_P, US_S = SH, 2 * SH + TP

R_BADA, R_GMIX, R_GFFN, R_BDW, R_LNG, R_LNB, R_WSH, R_GFIN, R_C = 0, 48, 56, 64, 68, 72, 76, 88, 96
NROWS = 112

SLOTS = 4
SLOT = 2 * DC * P
UNIT = SLOT
NP = (2 * T - NE) // P + NE
OUT_AT = (0, 1, 2, 3, 4, 5, 7, 9, EC)
CPP = 12 + len(OUT_AT) - 1
AHEAD = 4
GW = (512, 512, DFE - 1024)
NUNITS = 12


def plan():
    first, tmp, n, t = {}, {}, 0, 0
    stages = [("ada", 0, 24, 0), ("ada", 1, 24, 0)]
    for l in range(DEPTH):
        stages += [("qkv", l, 7, 0), ("glu", l, 4, 1), ("cxs", l, 4, 1), ("bgate", l, 2, 0), ("gates", l, 12, 0),
                   ("short", l, 4, 1), ("attn", l, 4, 1), ("conf", l, 4, 1), ("out", l, 4, 1)]
        if l % 2 == 0:
            stages += [("ffn_in", l, FC, 1), ("ffn_out", l, 2 * DC, 0.5)]
        else:
            stages += [("moe", l, CPP, 0)]
    for name, l, count, uses_tmp in stages:
        first[name, l], tmp[name, l] = n, t
        n += count
        t += int(count * uses_tmp)
    return first, tmp


def build(nc, x_prompt, x_sample, cache_k, cache_v, cache_idx_k, state_conv_conformer, state_conv_short,
          c_prompt, c_sample, w_ada, b_ada, g_norm_mix, g_norm_ffn, w_in, w_dw_conf, b_dw_conf,
          ln_conf_g, ln_conf_b, w_dw_short, w_branch, w_out, w_ffn_in, w_ffn_out, w_router, b_router,
          w_exp_in, w_exp_out, g_final,
          y_prompt, y_sample, pk, pv, pik, pconf, pshort, sk, sv, sik, sconf, sshort):
    first, tmp_before = plan()
    ADA_CHUNKS = 2 * 24

    with ExitStack() as ctx:
        def sb(name, shape, dt=F32):
            return ctx.enter_context(nc.sbuf_tensor(name, shape, dt))

        def sem(name):
            return ctx.enter_context(nc.semaphore(name))

        xT = sb("xT", [P, DC, T])
        tok = sb("tok", [P, 3 * D])
        ring = sb("ring", [P, SLOTS, SLOT])
        kTs = sb("kTs", [P, DEPTH, NKS])
        ikTs = sb("ikTs", [P, DEPTH, NKS])
        cv = sb("cv", [P, DEPTH, PAST // P, HD])
        tmp = sb("tmp", [P, 2, 2, T])
        hidf = sb("hidf", [P, 2, T])
        mean = sb("mean", [P, T])
        var = sb("var", [P, T])
        std = sb("std", [P, T])
        rstd = sb("rstd", [P, T])
        vec = sb("vec", [P, DEPTH, NROWS])
        dwc = sb("dwc", [P, DEPTH, CW * BC])
        cT = sb("cT", [P, DC, 2])
        mods = sb("mods", [P, DEPTH, 48, 2])
        gain = sb("gain", [P, DEPTH, 2, DC, 2])
        hist = sb("hist", [P, DEPTH, BC, CH + SH])
        ident = sb("ident", [P, P])
        ones = sb("ones", [P, P])
        top8 = sb("top8", [P, 8])
        iws = sb("iws", [P, 3, NH])
        nmax = sb("nmax", [P, 2])
        psums = sb("psums", [P, 2])
        prec = sb("prec", [P, 2])
        wr = sb("wr", [P, DC, NE])
        br = sb("br", [1, NE])
        iota_i = sb("iota_i", [P, P], I32)
        iota_f = sb("iota_f", [P, P])
        upper = sb("upper", [P, P])
        pass_i = sb("pass_i", [P, NP + 2], I32)
        wslot = sb("wslot", [P, 1])
        idx_u = sb("idx_u", [P, 8], U32)
        idx_f = sb("idx_f", [P, 8])
        rl = sb("rl", [P, 3, NE])
        comb = sb("comb", [P, 3, NE])
        comb2 = sb("comb2", [P, NE])
        rsc = sb("rsc", [P, 8])

        mixer = ctx.enter_context(ExitStack())

        def mb(name, shape, dt=F32):
            return mixer.enter_context(nc.sbuf_tensor(name, shape, dt))

        hT = mb("hT", [P, DC, T])
        merged = mb("merged", [P, DC, T])
        wide = mb("wide", [P, 3 * DC, T])
        qT = mb("qT", [P, 4, T])
        iqT = mb("iqT", [P, 4, TW])
        kT = mb("kT", [P, TW])
        ikT = mb("ikT", [P, TW])
        viwT = mb("viwT", [P, TW])
        u_conf = mb("u_conf", [P, BC, UCW])
        conv = mb("conv", [P, BC, UCW - CH])
        u_short = mb("u_short", [P, BC, USW])
        sconv = mb("sconv", [P, BC, USW - SH])
        bgate = mb("bgate", [P, BC, T])
        score = mb("score", [P, 960])
        work = mb("work", [P, 960])
        lm = mb("lm", [P, NKS])
        prob = mb("prob", [P, NKS])
        probT = mb("probT", [P, 2, 640])
        mixer.close()

        dense = ctx.enter_context(ExitStack())
        hid_lo = dense.enter_context(nc.sbuf_tensor("hid_lo", [P, FC, T], F32R))
        hid_hi = dense.enter_context(nc.sbuf_tensor("hid_hi", [P, FC, T], F32R))
        h_hi = dense.enter_context(nc.sbuf_tensor("h_hi", [P, DC, T], F32R))
        h_lo = dense.enter_context(nc.sbuf_tensor("h_lo", [P, DC, T], F32R))
        wd_hi = dense.enter_context(nc.sbuf_tensor("wd_hi", [P, 2, UNIT], F32R))
        wd_lo = dense.enter_context(nc.sbuf_tensor("wd_lo", [P, 2, UNIT], F32R))
        dense.close()

        experts = ctx.enter_context(ExitStack())

        def eb(name, shape, dt=F32):
            return experts.enter_context(nc.sbuf_tensor(name, shape, dt))

        hid_tok = eb("hid_tok", [P, DFE])
        y = eb("y", [P, D])
        eb("kept", [P, 2 * DC * T - DFE - D])
        S = eb("S", [P, 3, P])
        ST = eb("ST", [P, T])
        small = eb("small", [P, 820])
        xg_hi = eb("xg_hi", [P, DC, P], F32R)
        xg_lo = eb("xg_lo", [P, DC, P], F32R)
        hidT_hi = eb("hidT_hi", [P, EC, P], F32R)
        hidT_lo = eb("hidT_lo", [P, EC, P], F32R)
        we_hi = eb("we_hi", [P, AHEAD, UNIT], F32R)
        we_lo = eb("we_lo", [P, AHEAD, UNIT], F32R)
        experts.close()

        x_tok = tok[:, :].rearrange("p (t d) -> p t d", t=3)
        st_out = tok[:, 0:4 * DB].rearrange("p (s d) -> p s d", s=4)
        kvtok = tok[:, 4 * DB:4 * DB + 3 * 328].rearrange("p (t d) -> p t d", t=3)
        h_tok = x_tok
        wide_flat = wide[:, :, :].rearrange("p a b -> p (a b)")
        vrows = wide_flat[:, 0:DEPTH * 256].rearrange("p (l m c) -> p l m c", l=DEPTH, m=2)
        modrow = wide_flat[:, 4608:4608 + DEPTH * 1536].rearrange("p (l n) -> p l n", l=DEPTH)
        craw = wide_flat[:, 512:512 + DEPTH * 1024].rearrange("p (l m k c) -> p l m k c", l=DEPTH, m=2, k=4)
        hraw = wide_flat[:, 2560:2560 + DEPTH * 1024].rearrange("p (l m c) -> p l m c", l=DEPTH, m=2)
        NPT = NP + 1

        def table(at, *dims):
            n = int(np.prod(dims))
            v = small[:, at:at + n]
            return v if len(dims) == 1 else v.rearrange("p (a b) -> p a b", a=dims[0])

        member, rank = table(0, 3, NE), table(24, 3, NE)
        count, npass, cum = table(48, NE), table(56, NE), table(64, NE)
        ended, picked = table(80, NPT, NE), table(192, NPT, NE)
        pass_e, pass_start, pass_base = table(304, NPT), table(320, NPT), table(336, NPT)
        prod = small[:, 360:360 + 3 * NPT * NE].rearrange("p (t a e) -> p t a e", t=3, a=NPT)
        row_rank, row_in, row_w = table(700, 3, NPT), table(740, 3, NPT), table(780, 3, NPT)
        gates = wide
        attnT = iqT[:, :, 0:T]
        confT = qT
        shortT = u_short[:, :, :].rearrange("p a b -> p (a b)")[:, 0:BC * T].rearrange("p (a b) -> p a b", a=BC)
        rel = merged[:, :, :].rearrange("p a b -> p (a b)")[:, 0:1920].rearrange("p (a b) -> p a b", a=2)
        sq_mix = wide[:, 0:DC, :]
        sq_end = ring[:, :, :].rearrange("p a b -> p (a b)")[:, 0:DC * T].rearrange("p (a b) -> p a b", a=DC)

        def sq(k):
            return sq_end if k == 2 * DEPTH else sq_mix

        acc = merged

        mmp = ctx.enter_context(nc.psum_tensor("mmp", [P, 4, 512], F32))
        lg = ctx.enter_context(nc.psum_tensor("lg", [P, 1024], F32))
        px = ctx.enter_context(nc.psum_tensor("px", [P, 512], F32))
        py = ctx.enter_context(nc.psum_tensor("py", [P, 512], F32))

        consts_ready = sem("consts_ready")
        w_full = [sem(f"w_full{i}") for i in range(SLOTS)]
        chunk_done = sem("chunk_done")
        slot_free = [sem(f"slot_free{i}") for i in range(SLOTS)]
        hi_ready = sem("hi_ready")
        lo_ready = sem("lo_ready")
        hl_ready = sem("hl_ready")
        xg_split = sem("xg_split")
        hidT_split = sem("hidT_split")
        pair_evac = sem("pair_evac")
        tmp_ready = sem("tmp_ready")
        tmp_free = sem("tmp_free")
        rows_loaded = sem("rows_loaded")
        x_loaded = sem("x_loaded")
        caches_loaded = sem("caches_loaded")
        router_loaded = sem("router_loaded")
        pro_tr = sem("pro_tr")
        pro_copied = sem("pro_copied")
        c_ready = sem("c_ready")
        mods_ready = sem("mods_ready")
        x_ready = sem("x_ready")
        sq_ready = sem("sq_ready")
        sum_ready = sem("sum_ready")
        ms_ready = sem("ms_ready")
        std_ready = sem("std_ready")
        xn_step = sem("xn_step")
        xn_ready = sem("xn_ready")
        h_ready = sem("h_ready")
        kv_tr = sem("kv_tr")
        kv_copied = sem("kv_copied")
        sc_done = sem("sc_done")
        rel_ready = sem("rel_ready")
        rel_used = sem("rel_used")
        hist_ready = sem("hist_ready")
        u_ready = sem("u_ready")
        st_tr = sem("st_tr")
        st_copied = sem("st_copied")
        stored = sem("stored")
        lg_done = sem("lg_done")
        lm_done = sem("lm_done")
        exp_done = sem("exp_done")
        prob_ready = sem("prob_ready")
        pt_done = sem("pt_done")
        pt_copied = sem("pt_copied")
        av_done = sem("av_done")
        attn_copied = sem("attn_copied")
        short_ready = sem("short_ready")
        conv_ready = sem("conv_ready")
        ln_sum = sem("ln_sum")
        xc_ready = sem("xc_ready")
        ln_sq = sem("ln_sq")
        ln_ss = sem("ln_ss")
        ln_ms = sem("ln_ms")
        ln_std = sem("ln_std")
        ln_n = sem("ln_n")
        conf_ready = sem("conf_ready")
        merged_ready = sem("merged_ready")
        hid_ready = sem("hid_ready")
        hid_step = sem("hid_step")
        rt_done = sem("rt_done")
        rt_d = sem("rt_d")
        rt_e = sem("rt_e")
        comb_ready = sem("comb_ready")
        ada_evac = sem("ada_evac")
        mod_tr = sem("mod_tr")
        ht_tr = sem("ht_tr")
        ht_copied = sem("ht_copied")
        rank_done = sem("rank_done")
        passes_ready = sem("passes_ready")
        acc_zeroed = sem("acc_zeroed")
        tables_ready = sem("tables_ready")
        s_ready = sem("s_ready")
        xg_done = sem("xg_done")
        xg_ready = sem("xg_ready")
        silu_ready = sem("silu_ready")
        hg_ready = sem("hg_ready")
        hid_tr = sem("hid_tr")
        hidT_ready = sem("hidT_ready")
        st2_tr = sem("st2_tr")
        st2_ready = sem("st2_ready")
        yslot_ready = sem("yslot_ready")
        sc2_done = sem("sc2_done")
        sc2_added = sem("sc2_added")
        y_ready = sem("y_ready")
        y_tr = sem("y_tr")
        y_copied = sem("y_copied")
        y_stored = sem("y_stored")
        dve_step = sem("dve_step")
        pool_step = sem("pool_step")

        w3 = {"in": w_in.rearrange("l (c p) n -> l p c n", p=P),
              "ada": w_ada.rearrange("l (c p) n -> l p c n", p=P),
              "out": w_out.rearrange("l (c p) n -> l p c n", p=P),
              "branch": w_branch.rearrange("l b (c p) n -> l b p c n", p=P),
              "ffn_in": w_ffn_in.rearrange("l (c p) n -> l p c n", p=P),
              "ffn_out": w_ffn_out.rearrange("l (c p) n -> l p c n", p=P),
              "exp_in": w_exp_in.rearrange("l e (c p) n -> l e p c n", p=P),
              "exp_out": w_exp_out.rearrange("l e (c p) n -> l e p c n", p=P)}

        def slot_view(slot, k, n):
            return ring[:, slot, 0:k * n].rearrange("p (k n) -> p k n", k=k)

        def segs(buf, off_p, off_s):
            return [(buf[..., off_p:off_p + TP], slice(0, TP)), (buf[..., off_s:off_s + TS], slice(TP, T))]

        block = ctx.enter_context(nc.Block())

        @block.sync
        def _(sp):
            def load(n, parts, it=None, fills=1):
                if it is not None:
                    sp.wait_ge(slot_free[n % SLOTS], it * fills + n // SLOTS)
                elif n >= SLOTS:
                    sp.wait_ge(slot_free[n % SLOTS], n // SLOTS)
                assert len(parts) == 2
                for dst, src in parts:
                    sp.dma_start(dst, src).then_inc(w_full[n % SLOTS], 16)

            def halves(v, src, k):
                return [(v[:, 0:k // 2], src[:, 0:k // 2]), (v[:, k // 2:k], src[:, k // 2:k])]

            def cols(n, src, c0, k=DC, width=2 * P):
                return halves(slot_view(n % SLOTS, k, width), src[:, :, c0:c0 + width], k)

            def two_blocks(n, src, ca, cb, k=DC):
                v = slot_view(n % SLOTS, k, 2 * P)
                return [(v[:, :, 0:P], src[:, :, ca:ca + P]), (v[:, :, P:2 * P], src[:, :, cb:cb + P])]

            def dyn_cols(n, src, expr, k=DC, width=2 * P):
                return halves(slot_view(n % SLOTS, k, width), src[:, :, bass.ds(expr, width)], k)

            def dyn_two(n, src, expr, gap, k=DC):
                v = slot_view(n % SLOTS, k, 2 * P)
                return [(v[:, :, 0:P], src[:, :, bass.ds(expr, P)]), (v[:, :, P:2 * P], src[:, :, bass.ds(expr + gap, P)])]

            for l in range(DEPTH):
                n0 = first["ada", l]
                peel = SLOTS if l == 0 else 0
                for k in range(peel):
                    load(n0 + k, cols(n0 + k, w3["ada"][l], 2 * P * k))
                with sp.Fori(0, 24 // SLOTS - peel // SLOTS) as it:
                    for k in range(SLOTS):
                        n = n0 + peel + k
                        load(n, dyn_cols(n, w3["ada"][l], it * (SLOTS * 2 * P) + 2 * P * (k + peel)), it)

            for l in range(DEPTH):
                win = w3["in"][l]
                n = first["qkv", l]
                for i, c in enumerate((K0, IK0)):
                    v = slot_view((n + i) % SLOTS, DC, P)
                    load(n + i, [(v[:, :, r * HD:(r + 1) * HD], win[:, :, c:c + HD]) for r in range(2)])
                n += 1
                load(n + 1, cols(n + 1, win, IQ0))
                load(n + 2, cols(n + 2, win, IQ0 + 2 * P))
                v = slot_view((n + 3) % SLOTS, DC, 2 * P)
                load(n + 3, [(v[:, :, 0:HD], win[:, :, V0:V0 + HD]), (v[:, :, HD:HD + NH], win[:, :, IW0:IW0 + NH])])
                load(n + 4, cols(n + 4, win, Q0))
                load(n + 5, cols(n + 5, win, Q0 + 2 * P))
                for j in range(BC):
                    n = first["glu", l] + j
                    load(n, two_blocks(n, win, GLU0 + P * j, GLU0 + DB + P * j))
                for j in range(BC):
                    n = first["cxs", l] + j
                    load(n, two_blocks(n, win, SC0 + DB + P * j, SC0 + 2 * DB + P * j))
                for j in range(2):
                    n = first["bgate", l] + j
                    load(n, cols(n, win, SC0 + 2 * P * j))
                for j in range(12):
                    n = first["gates", l] + j
                    load(n, cols(n, win, GATE0 + 2 * P * j))
                for stage, b in (("short", 2), ("attn", 0), ("conf", 1)):
                    for j in range(4):
                        n = first[stage, l] + j
                        load(n, cols(n, w3["branch"][l, b], 2 * P * j, BC))
                for j in range(4):
                    n = first["out", l] + j
                    load(n, cols(n, w3["out"][l], 2 * P * j))
                if l % 2 == 0:
                    n0 = first["ffn_in", l]
                    with sp.Fori(0, FC // SLOTS) as it:
                        for k in range(SLOTS):
                            load(n0 + k, dyn_two(n0 + k, w3["ffn_in"][l // 2], it * (SLOTS * P) + P * k, DFF), it)
                    for k in range(FC - FC % SLOTS, FC):
                        load(n0 + k, two_blocks(n0 + k, w3["ffn_in"][l // 2], P * k, DFF + P * k))
                    n0 = first["ffn_out", l]
                    with sp.Fori(0, 2 * DC // SLOTS) as it:
                        for k in range(SLOTS):
                            v = slot_view((n0 + k) % SLOTS, EC, P)
                            src = w3["ffn_out"][l // 2][:, (k % 2) * EC:(k % 2 + 1) * EC,
                                                        bass.ds(it * (SLOTS * P // 2) + P * (k // 2), P)]
                            load(n0 + k, [(v[:, 0:6], src[:, 0:6]), (v[:, 6:EC], src[:, 6:EC])], it)
                else:
                    n0 = first["moe", l]
                    sp.wait_ge(passes_ready, 1)
                    total = sp.value_load(pass_i[0:1, NP + 1:NP + 2], min_val=5, max_val=NP)
                    fills = CPP // SLOTS

                    with sp.Fori(0, total) as p:
                        e = sp.value_load(pass_i[0:1, bass.ds(p, 1)], min_val=0, max_val=NE - 1)
                        win_e = w3["exp_in"][l // 2, bass.ds(e, 1)].rearrange("e p c n -> (e p) c n")
                        wout_e = w3["exp_out"][l // 2, bass.ds(e, 1)].rearrange("e p c n -> (e p) c n")
                        k = 0
                        for g, w in enumerate(GW):
                            for c0 in (512 * g, DFE + 512 * g):
                                for r in range(0, DC, 4):
                                    v = slot_view((n0 + k) % SLOTS, 4, w)
                                    load(n0 + k, halves(v, win_e[:, r:r + 4, c0:c0 + w], 4), p, fills)
                                    k += 1
                        for f, f1 in zip(OUT_AT, OUT_AT[1:]):
                            m = f1 - f
                            v = slot_view((n0 + k) % SLOTS, m, D)
                            src = wout_e[:, f:f + m, :]
                            load(n0 + k, [(v[:, :, h * 512:(h + 1) * 512], src[:, :, h * 512:(h + 1) * 512])
                                          for h in range(2)], p, fills)
                            k += 1
                    for k in range(AHEAD):
                        sp.wait_ge(slot_free[(n0 + k) % SLOTS], total * fills + (n0 + k) // SLOTS)
                        sp.sem_inc(w_full[(n0 + k) % SLOTS], 32)

        @block.gpsimd
        def _(pool):
            nc.gpsimd.memset(ident[:], 0.0).then_inc(pool_step, 1)
            nc.gpsimd.memset(ones[:], 1.0).then_inc(consts_ready, 1)
            nc.gpsimd.memset(modrow, 0.0).then_inc(consts_ready, 1)
            nc.gpsimd.memset(upper[:], 1.0).then_inc(pool_step, 1)
            nc.gpsimd.iota(iota_i[:], pattern=[[1, P]], base=0, channel_multiplier=0).then_inc(pool_step, 1)
            pool.wait_ge(pool_step, 3)
            nc.gpsimd.affine_select(out=upper[:], in_=upper[:], compare_op=ALU.is_gt, fill=0.0, base=0,
                                    pattern=[[1, P]], channel_multiplier=-1).then_inc(consts_ready, 1)
            nc.gpsimd.tensor_copy(iota_f[:], iota_i[:]).then_inc(consts_ready, 1)
            nc.gpsimd.affine_select(out=ident[:], in_=ident[:], compare_op=ALU.not_equal, fill=1.0, base=0,
                                    pattern=[[-1, P]], channel_multiplier=1).then_inc(consts_ready, 1)

            for l in range(DEPTH):
                pool.wait_ge(pro_copied, 14)
                if l > 0:
                    pool.wait_ge(x_ready, DC // 2 * (2 * l + 1))
                nc.gpsimd.memset(u_short[:, :, 0:SH], 0.0)
                nc.gpsimd.memset(u_conf[:, :, 0:CH], 0.0)
                nc.gpsimd.tensor_copy(u_conf[:, :, CH + TP:2 * CH + TP], hist[:, l, :, 0:CH])
                nc.gpsimd.tensor_copy(u_short[:, :, SH + TP:2 * SH + TP],
                                      hist[:, l, :, CH:CH + SH]).then_inc(hist_ready, 1)
                for stage, buf, op, os in (("glu", u_conf, UC_P, UC_S), ("cxs", u_short, US_P, US_S)):
                    for j in range(BC):
                        t = tmp_before[stage, l] + j
                        pool.wait_ge(tmp_ready, t + 1)
                        for dst, s in segs(buf[:, j, :], op, os):
                            ins = nc.gpsimd.tensor_tensor(dst, tmp[:, t % 2, 0, s], tmp[:, t % 2, 1, s], ALU.mult)
                        ins.then_inc(u_ready, 1)
                        pool.wait_ge(u_ready, 8 * l + 4 * (stage == "cxs") + j + 1)
                        nc.gpsimd.sem_inc(tmp_free, 1)

            pool.wait_ge(sum_ready, 2 * DEPTH)
            nc.gpsimd.memset(acc[:], 0.0).then_inc(acc_zeroed, 1)

        @block.tensor
        def _(pe):
            def group(out, pairs, **kw):
                for i, (a, b) in enumerate(pairs):
                    ins = nc.tensor.matmul(out, a, b, start=(i == 0), stop=(i == len(pairs) - 1), **kw)
                return ins

            def w_wait(n, it=None):
                if it is None:
                    pe.wait_ge(w_full[n % SLOTS], 32 * (n // SLOTS + 1))
                else:
                    pe.wait_ge(w_full[n % SLOTS], it * 32 + 32 * (n // SLOTS + 1))

            def pair_wait(n, it=None, per=SLOTS):
                need = n - ADA_CHUNKS - 1
                if it is not None:
                    pe.wait_ge(pair_evac, it * per + need)
                elif need >= 1:
                    pe.wait_ge(pair_evac, need)

            def pair_chunk(n, rhs, k=DC, blocks=((0, P), (P, P)), it=None, each=None, width=2 * P):
                w_wait(n, it)
                pair_wait(n, it)
                v = slot_view(n % SLOTS, k, width)
                for b, (c0, m) in enumerate(blocks):
                    for i in range(k):
                        if each is not None and b == 0:
                            each(i)
                        ins = nc.tensor.matmul(mmp[0:m, 2 * (n % 2) + b, 0:T], v[:, i, c0:c0 + m], rhs(i),
                                               start=(i == 0), stop=(i == k - 1))
                ins.then_inc(chunk_done, 1)

            def norm_sums(k, blocks=range(DC)):
                for c in blocks:
                    if c % 2 == 0:
                        pe.wait_ge(sq_ready, DC // 2 * k + c // 2 + 1)
                    ins = nc.tensor.matmul(py[:, 0:T], ones[:], sq(k)[:, c, :], start=(c == 0), stop=(c == DC - 1))
                if c == DC - 1:
                    ins.then_inc(sum_ready, 1)

            def h_rhs(i):
                return hT[:, i, :]

            def h_each(k):
                return lambda i: pe.wait_ge(h_ready, DC * k + i + 1)

            batch = [0]

            def pro(trs):
                b = batch[0]
                batch[0] += 1
                if b >= 4:
                    pe.wait_ge(pro_copied, b - 3)
                for out, in_, k in trs(mmp[:, b % 4, :]):
                    ins = nc.tensor.transpose(out, in_, ident[0:k, 0:k])
                ins.then_inc(pro_tr, 1)

            pe.wait_ge(consts_ready, 5)
            pe.wait_ge(rows_loaded, 16 * 26)
            for l in range(DEPTH):
                pro(lambda b: [(b[:, 0:NROWS], vrows[0:NROWS, l, 0, :], NROWS),
                               (b[:, P:P + CW * BC], vrows[0:CW * BC, l, 1, :], CW * BC)])

            def pro_rest():
                pe.wait_ge(x_loaded, 32)
                for t in range(3):
                    m = P if t < 2 else TS
                    for g in range(2):
                        pro(lambda b: [(b[:, j * P:j * P + m], x_tok[0:m, t, (4 * g + j) * P:(4 * g + j + 1) * P], m)
                                       for j in range(4)])
                pe.wait_ge(caches_loaded, 16 * 14)
                for l in range(DEPTH):
                    for m in range(2):
                        pro(lambda b: [(b[:, j * P:(j + 1) * P], craw[:, l, m, j, :], P) for j in range(4)])
                    pro(lambda b: [(b[:, j * 32:j * 32 + CH], hraw[0:CH, l, 0, j * P:(j + 1) * P], CH) for j in range(4)]
                        + [(b[:, j * 32 + CH:j * 32 + 32], hraw[0:SH, l, 1, j * P:(j + 1) * P], SH) for j in range(4)])

            pe.wait_ge(c_ready, 1)
            pe.wait_ge(pro_copied, 2)

            for l in range(DEPTH):
                n0 = first["ada", l]
                if l == 1:
                    pro_rest()
                    pe.wait_ge(pro_copied, 14)
                with pe.Fori(0, 24 // SLOTS) as it:
                    for k in range(SLOTS):
                        n = n0 + k
                        w_wait(n, it)
                        pe.wait_ge(ada_evac, it * SLOTS + (n + 1))
                        v = slot_view(n % SLOTS, DC, 2 * P)
                        ins = group(mmp[32 * k:32 * k + 2, k, 0:2 * P], [(cT[:, i, :], v[:, i, :]) for i in range(DC)])
                        ins.then_inc(chunk_done, 1)
                pe.wait_ge(ada_evac, n0 + 24 + SLOTS)
                for b in range(3):
                    bank = (lg[:, 0:512], lg[:, 512:1024], px)[b]
                    if l:
                        pe.wait_ge(mods_ready, 1)
                    for q in range(4):
                        ins = nc.tensor.transpose(bank[:, q * P:(q + 1) * P],
                                                  modrow[:, l, (4 * b + q) * P:(4 * b + q + 1) * P], ident[:])
                    ins.then_inc(mod_tr, 1)

            for l in range(DEPTH):
                norm_sums(2 * l)
                n = first["qkv", l]
                pair_chunk(n, h_rhs, blocks=((0, P),), width=P, each=h_each(2 * l))
                pair_chunk(n + 1, h_rhs, blocks=((0, P),), width=P)
                n += 1
                pair_chunk(n + 1, h_rhs)
                pair_chunk(n + 2, h_rhs)
                pair_chunk(n + 3, h_rhs, blocks=((0, HD + NH),))

                pe.wait_ge(pair_evac, n + 3 - ADA_CHUNKS + 1)
                for t in range(3):
                    bank = (lg[:, 0:512], lg[:, 512:1024], px)[t]
                    for dst, src, k in ((0, kT, P), (P, ikT, P), (2 * P, viwT, HD + NH)):
                        ins = nc.tensor.transpose(bank[:, dst:dst + k], src[0:k, t * P:(t + 1) * P], ident[0:k, 0:k])
                    ins.then_inc(kv_tr, 1)

                def score_head(h):
                    s = slice(HD * (h % 2), HD * (h % 2) + HD)
                    if h == 0:
                        pe.wait_ge(kv_copied, 3 * (l + 1))
                    pe.wait_ge(rel_ready, 8 * l + h)
                    q = iqT[s, h // 2, :]
                    nc.tensor.matmul(px[:, 0:P], q[:, 0:P], ikT[s, 0:P], start=True, stop=True)
                    nc.tensor.matmul(py[:, 0:TP], q[:, P:TP], ikT[s, 0:TP], start=True, stop=True)
                    qs = q[:, TP:TP + 2 * TS]
                    nc.tensor.matmul(lg[:, 0:PAST], qs, ikTs[s, l, 0:PAST], start=True, stop=True)
                    nc.tensor.matmul(lg[:, PAST:NKS], qs, ikTs[s, l, PAST:NKS], start=True,
                                     stop=True).then_inc(sc_done, 1)

                order = [first["qkv", l] + 5, first["qkv", l] + 6] + [first["glu", l] + j for j in range(4)] \
                    + [first["cxs", l] + j for j in range(4)]
                for h, n in enumerate(order):
                    if h < NH:
                        score_head(h)
                    pair_chunk(n, h_rhs)
                for j in range(2):
                    pair_chunk(first["bgate", l] + j, h_rhs)

                pe.wait_ge(u_ready, 8 * (l + 1))
                pe.wait_ge(rel_ready, 8 * (l + 1))
                for s, (buf, c0, w) in enumerate(((u_conf, UC_P + TP - CH, CH), (u_conf, UC_S + TS - CH, CH),
                                                  (u_short, US_P + TP - SH, SH), (u_short, US_S + TS - SH, SH))):
                    bank = (lg[:, 0:512], lg[:, 512:1024], px, py)[s]
                    for j in range(BC):
                        ins = nc.tensor.transpose(bank[0:w, j * P:(j + 1) * P], buf[:, j, c0:c0 + w], ident[:])
                    ins.then_inc(st_tr, 1)

                def logits(u):
                    g = NUNITS * l + u
                    pe.wait_ge(lm_done, g) if g else None
                    if u < 8:
                        t, p, keys = u // 4, u % 4, P * (u // 4 + 1)
                        for h in range(2):
                            s = slice(HD * h, HD * h + HD)
                            ins = nc.tensor.matmul(lg[:, h * 512:h * 512 + keys], qT[s, p, t * P:(t + 1) * P],
                                                   kT[s, 0:keys], start=True, stop=True)
                    else:
                        for h in range(2):
                            s = slice(HD * h, HD * h + HD)
                            for a, b in ((0, PAST), (PAST, NKS)):
                                ins = nc.tensor.matmul(lg[s, a:b], qT[s, u - 8, TP:T], kTs[s, l, a:b],
                                                       start=True, stop=True)
                    ins.then_inc(lg_done, 1)

                def transposes(u):
                    g = NUNITS * l + u
                    pe.wait_ge(prob_ready, g + 1)
                    if g:
                        pe.wait_ge(pt_copied, g)
                    if u >= 8:
                        pe.wait_ge(attn_copied, g)
                    n_full = 2 * (u // 4 + 1) if u < 8 else 4
                    for i in range(n_full):
                        ins = nc.tensor.transpose(px[:, i * P:(i + 1) * P], prob[:, i * P:(i + 1) * P], ident[:])
                    if u >= 8:
                        ins = nc.tensor.transpose(py[0:TS, 3 * P:4 * P], prob[:, PAST:NKS], ident[:])
                    ins.then_inc(pt_done, 1)

                def values(u):
                    g = NUNITS * l + u
                    pe.wait_ge(pt_copied, g + 1)
                    if g:
                        pe.wait_ge(attn_copied, g)
                    for h in range(2):
                        s = slice(HD * h, HD * h + HD)
                        if u < 8:
                            nk = u // 4 + 1
                            ins = group(py[s, 0:P], [(kvtok[:, kc, 2 * P:2 * P + HD],
                                                      probT[:, u % 2, (h * nk + kc) * P:(h * nk + kc + 1) * P])
                                                     for kc in range(nk)])
                        else:
                            c = HD * h
                            prs = [(cv[:, l, kc, :], probT[:, u % 2, kc * P + c:kc * P + c + TS]) for kc in range(4)]
                            prs.append((kvtok[0:TS, 2, 2 * P:2 * P + HD], probT[0:TS, u % 2, 4 * P + c:4 * P + c + TS]))
                            ins = group(py[s, 0:TS], prs)
                    ins.then_inc(av_done, 1)

                pe.wait_ge(st_copied, 4 * (l + 1))

                def unit_tick(t):
                    if 0 <= t - 2 < NUNITS:
                        values(t - 2)
                    if 0 <= t < NUNITS:
                        logits(t)
                    if 0 <= t - 1 < NUNITS:
                        transposes(t - 1)

                for j in range(12):
                    unit_tick(j - 2)
                    pair_chunk(first["gates", l] + j, h_rhs)
                for j in range(4):
                    unit_tick(10 + j)
                    if j == 0:
                        pe.wait_ge(short_ready, l + 1)
                    pair_chunk(first["short", l] + j, lambda i: shortT[:, i, :], BC)

                for j in range(4):
                    if j == 0:
                        pe.wait_ge(conv_ready, l + 1)
                        group(px[:, 0:TP], [(ones[:], conv[:, c, 0:TP]) for c in range(BC)])
                        group(px[:, TP:T], [(ones[:], conv[:, c, UC_S - CH:UC_S - CH + TS])
                                            for c in range(BC)]).then_inc(ln_sum, 1)
                        pe.wait_ge(attn_copied, NUNITS * (l + 1))
                    if j == 1:
                        pe.wait_ge(ln_sq, l + 1)
                        group(py[:, 0:T], [(ones[:], hT[:, BC + c, :]) for c in range(BC)]).then_inc(ln_ss, 1)
                    pair_chunk(first["attn", l] + j, lambda i: attnT[:, i, :], BC)
                for j in range(4):
                    pair_chunk(first["conf", l] + j, lambda i: confT[:, i, :], BC,
                               each=(lambda i: pe.wait_ge(conf_ready, BC * l + i + 1)) if j == 0 else None)
                for j in range(4):
                    pair_chunk(first["out", l] + j, lambda i: merged[:, i, :],
                               each=(lambda i: pe.wait_ge(merged_ready, 4 * l + i // 2 + 1)) if j == 0 else None)
                    if j >= 1:
                        norm_sums(2 * l + 1, (2 * j - 2, 2 * j - 1))

                norm_sums(2 * l + 1, (DC - 2, DC - 1))
                if l % 2 == 0:
                    def split_chunk(n, s, x_hi, x_lo, k, blocks, bank, first_k=0, last_k=None, it=None, each=None):
                        pe.wait_ge(lo_ready, s + 1 if it is None else it * SLOTS + (s + 1))
                        pair_wait(n, it)
                        width = P * blocks
                        hi, lo = (w[:, s % 2, 0:k * width].rearrange("p (k n) -> p k n", k=k) for w in (wd_hi, wd_lo))
                        for b in range(blocks):
                            out = mmp[:, bank + b, 0:T]
                            for i in range(k):
                                if each is not None and b == 0:
                                    each(i)
                                c = slice(b * P, (b + 1) * P)
                                nc.tensor.matmul(out, hi[:, i, c], x_hi(i), start=(i + first_k == 0), stop=False)
                                nc.tensor.matmul(out, hi[:, i, c], x_lo(i), start=False, stop=False)
                                ins = nc.tensor.matmul(out, lo[:, i, c], x_hi(i), start=False,
                                                       stop=(i + first_k == (last_k or k - 1)))
                        ins.then_inc(chunk_done, 1)

                    def ffn_in(n, s, it=None, each=None):
                        split_chunk(n, s, lambda i: h_hi[:, i, :], lambda i: h_lo[:, i, :], DC, 2, 2 * (n % 2),
                                    it=it, each=each)

                    def ffn_out(k, it=None):
                        h = k % 2
                        split_chunk(first["ffn_out", l] + k, FC + k, lambda i: hid_hi[:, h * EC + i, :],
                                    lambda i: hid_lo[:, h * EC + i, :], EC, 1, 2 * ((k // 2 + first["ffn_out", l]) % 2), h * EC, FC - 1, it)

                    n0, peel = first["ffn_in", l], FC % SLOTS
                    for k in range(peel):
                        ffn_in(n0 + k, k, each=(lambda i: pe.wait_ge(hl_ready, i + 1)) if k == 0 else None)
                    with pe.Fori(0, FC // SLOTS) as it:
                        for k in range(peel, SLOTS + peel):
                            ffn_in(n0 + k, k, it)
                    pe.wait_ge(hid_ready, EC)
                    with pe.Fori(0, 2 * DC // SLOTS) as it:
                        for k in range(SLOTS):
                            if k == 1:
                                pe.wait_ge(hid_ready, FC)
                            ffn_out(k, it)
                else:
                    for c in range(DC):
                        pe.wait_ge(h_ready, DC * (2 * l + 1) + c + 1)
                    pe.wait_ge(router_loaded, 32)
                    for t in range(3):
                        m = P if t < 2 else TS
                        ts = slice(t * P, t * P + m)
                        ins = group(px[0:m, t * NE:(t + 1) * NE],
                                    [(hT[:, c, ts], wr[:, c, :]) for c in range(DC)] + [(ones[0:1, 0:m], br[0:1, :])])
                    ins.then_inc(rt_done, 1)
                    for b in range(6):
                        t, g = b // 2, b % 2
                        m = P if t < 2 else TS
                        if b >= 4:
                            pe.wait_ge(ht_copied, b - 3)
                        for j in range(4):
                            ins = nc.tensor.transpose(mmp[0:m, b % 4, j * P:(j + 1) * P],
                                                      hT[:, 4 * g + j, t * P:t * P + m], ident[:])
                        ins.then_inc(ht_tr, 1)
                    pe.wait_ge(comb_ready, 1)
                    rows = (P, P, TS)
                    for t in range(3):
                        m = rows[t]
                        group(py[0:m, t * NE:(t + 1) * NE], [(upper[0:m, 0:m], member[0:m, t, :])]
                              + [(ones[:, 0:m], member[:, b, :]) for b in range(t)])
                    group(py[:, 3 * NE:4 * NE], [(ones[0:rows[t], :], member[0:rows[t], t, :])
                                                 for t in range(3)]).then_inc(rank_done, 1)

                    pe.wait_ge(tables_ready, 1)
                    total = pe.value_load(pass_i[0:1, NP + 1:NP + 2], min_val=5, max_val=NP)

                    def gather(blocks):
                        for c in blocks:
                            ins = group(lg[:, c * P:(c + 1) * P],
                                        [(h_tok[0:rows[t], t, c * P:(c + 1) * P], S[0:rows[t], t, :])
                                         for t in range(3)])
                        if c == DC - 1:
                            ins.then_inc(xg_done, 1)

                    scatter_banks = (lg[:, 0:T], lg[:, 512:512 + T], px[:, 0:T], py[:, 0:T])

                    def scatter(done, blocks=range(DC)):
                        for c in blocks:
                            if c >= 4:
                                pe.wait_ge(sc2_added, done + (c - 3))
                            nc.tensor.matmul(scatter_banks[c % 4], y[:, c * P:(c + 1) * P], ST[:], start=True,
                                             stop=True).then_inc(sc2_done, 1)

                    def hid_transposes(b):
                        bank = (px, py, px)[b]
                        for f in range(4 * b, min(4 * b + 4, EC)):
                            ins = nc.tensor.transpose(bank[:, (f % 4) * P:(f % 4 + 1) * P],
                                                      hid_tok[:, f * P:(f + 1) * P], ident[:])
                        ins.then_inc(hid_tr, 1)

                    S0 = FC + 2 * DC
                    pe.wait_ge(ht_copied, 6)
                    pe.wait_ge(s_ready, 1)
                    gather(range(DC))
                    n0 = first["moe", l]
                    with pe.Fori(0, total) as p:
                        def weights(k, rows_k, w):
                            pe.wait_ge(lo_ready, p * CPP + (S0 + k + 1))
                            return [x[:, k % AHEAD, 0:rows_k * w].rearrange("p (k n) -> p k n", k=rows_k)
                                    for x in (we_hi, we_lo)]

                        def three(bank, x_hi, x_lo, w_hi, w_lo, is_first, is_last):
                            nc.tensor.matmul(bank, x_hi, w_hi, start=is_first, stop=False)
                            nc.tensor.matmul(bank, x_hi, w_lo, start=False, stop=False)
                            return nc.tensor.matmul(bank, x_lo, w_hi, start=False, stop=is_last)

                        pe.wait_ge(xg_split, p + 1)
                        k = 0
                        for g, w in enumerate(GW):
                            for role in range(2):
                                bank = mmp[:, 2 * (g % 2) + role, 0:w]
                                if role == 0:
                                    if g == 1:
                                        pe.wait_ge(yslot_ready, p + 1)
                                    if g == 2:
                                        pe.wait_ge(hg_ready, p * 3 + 1)
                                for r in range(0, DC, 4):
                                    hi, lo = weights(k, 4, w)
                                    for i in range(4):
                                        ins = three(bank, xg_hi[:, r + i, :], xg_lo[:, r + i, :], hi[:, i, :],
                                                    lo[:, i, :], r + i == 0, r + i == DC - 1)
                                    ins.then_inc(chunk_done, 1)
                                    k += 1
                                    if k == 3:
                                        pe.wait_ge(yslot_ready, p + 1)
                                    if 3 <= k < 7:
                                        scatter(p * DC, (2 * (k - 3), 2 * (k - 3) + 1))
                                    if k == 8:
                                        pe.wait_ge(sc2_added, p * DC + DC)
                                        for t in range(3):
                                            nc.tensor.transpose(py[:, t * P:t * P + rows[t]], S[0:rows[t], t, :],
                                                                ident[0:rows[t], 0:rows[t]])
                                        group(px[:, 0:1], [(S[0:rows[t], t, :], row_w[0:rows[t], t, bass.ds(p, 1)])
                                                           for t in range(3)]).then_inc(st2_tr, 1)
                                    if k == 10:
                                        pe.wait_ge(st2_ready, p + 1)
                                        pe.wait_ge(hg_ready, p * 3 + 2)
                                        hid_transposes(0)
                                        hid_transposes(1)
                        for f0, f1 in zip(OUT_AT, OUT_AT[1:]):
                            hi, lo = weights(k, f1 - f0, D)
                            for f in range(f0, f1):
                                if f % 4 == 0:
                                    pe.wait_ge(hidT_split, p * 3 + (f // 4 + 1))
                                for h in range(2):
                                    c = slice(h * 512, (h + 1) * 512)
                                    ins = three(mmp[:, 2 + h, :], hidT_hi[:, f, :], hidT_lo[:, f, :],
                                                hi[:, f - f0, c], lo[:, f - f0, c], f == 0, f == EC - 1)
                            ins.then_inc(chunk_done, 1)
                            k += 1
                            if k == 13:
                                pe.wait_ge(s_ready, p + 2)
                            if k == 14:
                                pe.wait_ge(hg_ready, p * 3 + 3)
                                hid_transposes(2)
                            if k <= 16:
                                gather((2 * (k - 13), 2 * (k - 13) + 1))
                    pe.wait_ge(yslot_ready, total + 1)
                    pe.wait_ge(xg_split, total + 1)
                    scatter(total * DC)
                    pe.wait_ge(sc2_added, total * DC + DC)

            norm_sums(4)
            pe.wait_ge(h_ready, DC * 5)
            for b in range(6):
                t, g = b // 2, b % 2
                m = P if t < 2 else TS
                if b >= 4:
                    pe.wait_ge(y_copied, b - 3)
                for j in range(4):
                    ins = nc.tensor.transpose(mmp[0:m, b % 4, j * P:(j + 1) * P], hT[:, 4 * g + j, t * P:t * P + m],
                                              ident[:])
                ins.then_inc(y_tr, 1)

        @block.scalar
        def _(act):
            copy = nc.scalar.copy

            for l in range(DEPTH):
                v = vrows[:, l, 0, :]
                for row, ap, k in ((R_BADA, b_ada[l], 48), (R_GMIX, g_norm_mix[l], 8), (R_GFFN, g_norm_ffn[l], 8),
                                   (R_BDW, b_dw_conf[l], 4), (R_LNG, ln_conf_g[l], 4), (R_LNB, ln_conf_b[l], 4),
                                   (R_GFIN, g_final, 8), (R_C, c_prompt[0], 8), (R_C + 8, c_sample[0], 8)):
                    act.dma_start(v[row:row + k, :], ap.rearrange("(c p) -> c p", p=P)).then_inc(rows_loaded, 16)
                for w in range(SW):
                    act.dma_start(v[R_WSH + 4 * w:R_WSH + 4 * w + 4, :],
                                  w_dw_short[l, w].rearrange("(c p) -> c p", p=P)).then_inc(rows_loaded, 16)
                act.dma_start(vrows[0:CW * BC, l, 1, :],
                              w_dw_conf[l].rearrange("w (c p) -> (w c) p", p=P)).then_inc(rows_loaded, 16)
            act.dma_start(x_tok[:, 0:2, :], x_prompt[0].rearrange("(t p) d -> p t d", p=P)).then_inc(x_loaded, 16)
            act.dma_start(x_tok[0:TS, 2, :], x_sample[0]).then_inc(x_loaded, 16)
            for l in range(DEPTH):
                for m, cache in enumerate((cache_k, cache_idx_k)):
                    src = cache[l, 0].rearrange("(k p) d -> p k d", p=P)
                    for r in range(2):
                        act.dma_start(craw[:, l, m, :, r * HD:(r + 1) * HD], src).then_inc(caches_loaded, 16)
                act.dma_start(hraw[0:CH, l, 0, :], state_conv_conformer[l, 0]).then_inc(caches_loaded, 16)
                act.dma_start(hraw[0:SH, l, 1, :], state_conv_short[l, 0]).then_inc(caches_loaded, 16)
                act.dma_start(cv[:, l, :, :], cache_v[l, 0].rearrange("(k p) d -> p k d", p=P)).then_inc(caches_loaded, 16)
            act.dma_start(wr[:], w_router[0].rearrange("(c p) e -> p c e", p=P)).then_inc(router_loaded, 16)
            act.dma_start(br[:], b_router[0:1, :]).then_inc(router_loaded, 16)

            act.wait_ge(pro_copied, 1)
            for s in range(2):
                ins = nc.scalar.activation(cT[:, :, s], vec[:, 0, R_C + 8 * s:R_C + 8 * s + 8], ACT.Silu)
            ins.then_inc(c_ready, 1)

            act.wait_ge(consts_ready, 5)
            act.sem_inc(ada_evac, SLOTS)
            for l in range(DEPTH):
                n0 = first["ada", l]
                with act.Fori(0, 24 // SLOTS) as it:
                    for k in range(SLOTS):
                        act.wait_ge(chunk_done, it * SLOTS + (n0 + k + 1))
                        act.sem_inc(slot_free[(n0 + k) % SLOTS], 1)
                        rows = slice(32 * k, 32 * k + 2)
                        copy(modrow[rows, l, bass.ds(it * 256, 256)], mmp[rows, k, 0:256]).then_inc(ada_evac, 1)

            def square(k, j):
                act.wait_ge(x_ready, DC // 2 * k + j + 1)
                c = slice(2 * j, 2 * j + 2)
                nc.scalar.activation(sq(k)[:, c, :], xT[:, c, :], ACT.Square).then_inc(sq_ready, 1)

            def norm(k, gain_of, shift_of, meanwhile=None, pairs=range(DC // 2)):
                for j in pairs:
                    square(k, j)
                if meanwhile is not None:
                    meanwhile()
                act.wait_ge(ms_ready, k + 1)
                nc.scalar.activation(std[:], var[:], ACT.Sqrt).then_inc(std_ready, 1)
                for c in range(DC):
                    act.wait_ge(xn_ready, DC * k + c + 1)
                    b = shift_of(c)
                    nc.scalar.activation(hT[:, c, 0:TP], hT[:, c, 0:TP], ACT.Identity, scale=gain_of(c),
                                         bias=0.0 if b is None else b).then_inc(h_ready, 1)

            def chunk_wait(n, it=None, split=False):
                act.wait_ge(chunk_done, n + 1 if it is None else it * SLOTS + (n + 1))
                if not split:
                    act.sem_inc(slot_free[n % SLOTS], 1)

            def split_high(n, s, dst, size, it=None, turn=None, fills=1, depth=2):
                full = 32 * (n // SLOTS + 1)
                act.wait_ge(w_full[n % SLOTS], full if it is None else it * (32 * fills) + full)
                if it is not None or s >= depth:
                    act.wait_ge(chunk_done, (n - depth + 1) if it is None else it * turn + (n - depth + 1))
                copy(dst, ring_flat(n, size)).then_inc(hi_ready, 1)

            def ring_flat(n, size):
                return ring[:, n % SLOTS, 0:size]

            def pair(n, b, m=P):
                return mmp[0:m, 2 * (n % 2) + b, 0:T]

            def to_tmp(n, t, f0, f1, it=None, split=False):
                chunk_wait(n, it, split)
                if it is not None:
                    act.wait_ge(tmp_free, it * SLOTS + (t - 1))
                elif t >= 2:
                    act.wait_ge(tmp_free, t - 1)
                ins = nc.scalar.activation(tmp[:, t % 2, 0, :], pair(n, 0), f0)
                if f1 is not None:
                    ins = nc.scalar.activation(tmp[:, t % 2, 1, :], pair(n, 1), f1)
                ins.then_inc(tmp_ready, 1)
                act.wait_ge(tmp_ready, (t + 1) if it is None else it * SLOTS + (t + 1))
                act.sem_inc(pair_evac, 1)

            for l in range(DEPTH):
                def gain_of(which):
                    return lambda c: gain[:, l, which, c, 0:1]

                def shift_of(which):
                    return lambda c: mods[:, l, 24 * which + c, 0:1]

                norm(2 * l, gain_of(0), shift_of(0), (lambda: act.wait_ge(mods_ready, DEPTH)) if l == 0 else None)

                n = first["qkv", l]
                chunk_wait(n)
                copy(kT[:, 0:T], pair(n, 0))
                copy(kT[:, T:TW], pair(n, 0)[:, TP:T])
                copy(kTs[:, l, PAST:NKS], pair(n, 0)[:, TP:T]).then_inc(pair_evac, 1)
                n += 1
                chunk_wait(n)
                copy(ikT[:, 0:T], pair(n, 0))
                copy(ikT[:, T:TW], pair(n, 0)[:, TP:T])
                copy(ikTs[:, l, PAST:NKS], pair(n, 0)[:, TP:T]).then_inc(pair_evac, 1)
                for j in range(2):
                    chunk_wait(n + 1 + j)
                    for b in range(2):
                        copy(iqT[:, 2 * j + b, 0:T], pair(n + 1 + j, b))
                        ins = copy(iqT[:, 2 * j + b, T:TW], pair(n + 1 + j, b)[:, TP:T])
                    ins.then_inc(pair_evac, 1)
                chunk_wait(n + 3)
                copy(viwT[0:HD + NH, 0:T], pair(n + 3, 0, HD + NH))
                copy(viwT[0:HD + NH, T:TW], pair(n + 3, 0, HD + NH)[:, TP:T]).then_inc(pair_evac, 1)

                if l:
                    act.wait_ge(stored, 16 * 10 * l)
                for t in range(3):
                    act.wait_ge(kv_tr, 3 * l + t + 1)
                    bank = (lg[:, 0:512], lg[:, 512:1024], px)[t]
                    copy(kvtok[:, t, :], bank[:, 0:328]).then_inc(kv_copied, 1)
                act.wait_ge(kv_copied, 3 * (l + 1))
                for dst_p, dst_s, c0 in ((pk, sk, 0), (pik, sik, P), (pv, sv, 2 * P)):
                    act.dma_start(dst_p[l, 0].rearrange("(t p) d -> p t d", p=P),
                                  kvtok[:, 0:2, c0:c0 + HD]).then_inc(stored, 16)
                    act.dma_start(dst_s[l, 0], kvtok[0:TS, 2, c0:c0 + HD]).then_inc(stored, 16)

                def relu_head(h):
                    g = 8 * l + h
                    act.wait_ge(sc_done, g + 1)
                    if g >= 2:
                        act.wait_ge(rel_used, g - 1)
                    nc.scalar.activation(rel[:, h % 2, 0:P], px[:, 0:P], ACT.Relu, scale=HD ** -0.5)
                    nc.scalar.activation(rel[:, h % 2, P:P + TP], py[:, 0:TP], ACT.Relu, scale=HD ** -0.5)
                    nc.scalar.activation(rel[:, h % 2, P + TP:960], lg[:, 0:NKS], ACT.Relu,
                                         scale=HD ** -0.5).then_inc(rel_ready, 1)

                for h in range(10):
                    if h < NH:
                        relu_head(h)
                    if h < 2:
                        n = first["qkv", l] + 5 + h
                        chunk_wait(n)
                        copy(qT[:, 2 * h, :], pair(n, 0))
                        copy(qT[:, 2 * h + 1, :], pair(n, 1)).then_inc(pair_evac, 1)
                    elif h < 6:
                        to_tmp(first["glu", l] + h - 2, tmp_before["glu", l] + h - 2, ACT.Copy, ACT.Sigmoid)
                    else:
                        to_tmp(first["cxs", l] + h - 6, tmp_before["cxs", l] + h - 6, ACT.Copy, ACT.Copy)
                for j in range(2):
                    n = first["bgate", l] + j
                    chunk_wait(n)
                    copy(bgate[:, 2 * j, :], pair(n, 0))
                    copy(bgate[:, 2 * j + 1, :], pair(n, 1)).then_inc(pair_evac, 1)

                for s, (w, dst) in enumerate(((CH, pconf), (CH, sconf), (SH, pshort), (SH, sshort))):
                    act.wait_ge(st_tr, 4 * l + s + 1)
                    bank = (lg[:, 0:512], lg[:, 512:1024], px, py)[s]
                    copy(st_out[0:w, s, :], bank[0:w, :]).then_inc(st_copied, 1)
                    act.wait_ge(st_copied, 4 * l + s + 1)
                    act.dma_start(dst[l, 0], st_out[0:w, s, :]).then_inc(stored, 16)

                def attn_copy(u):
                    act.wait_ge(av_done, NUNITS * l + u + 1)
                    if u < 8:
                        dst, src = attnT[:, u % 4, (u // 4) * P:(u // 4 + 1) * P], py[:, 0:P]
                    else:
                        dst, src = attnT[:, u - 8, TP:T], py[:, 0:TS]
                    copy(dst, src).then_inc(attn_copied, 1)

                def pt_copy(u):
                    g = NUNITS * l + u
                    act.wait_ge(pt_done, g + 1)
                    if g >= 2:
                        act.wait_ge(av_done, g - 1)
                    w = 2 * P * (u // 4 + 1) if u < 8 else 4 * P
                    ins = copy(probT[:, u % 2, 0:w], px[:, 0:w])
                    if u >= 8:
                        ins = copy(probT[0:TS, u % 2, 4 * P:5 * P], py[0:TS, 3 * P:4 * P])
                    ins.then_inc(pt_copied, 1)

                def exp(u):
                    g = NUNITS * l + u
                    act.wait_ge(lm_done, g + 1)
                    if g:
                        act.wait_ge(pt_done, g)
                    if u < 8:
                        keys = P * (u // 4 + 1)
                        for h in range(2):
                            s = slice(h * keys, (h + 1) * keys)
                            ins = nc.scalar.activation(prob[:, s], lm[:, s], ACT.Exp, bias=nmax[:, h:h + 1],
                                                       accum_out=psums[:, h:h + 1])
                    else:
                        ins = nc.scalar.activation(prob[:, 0:NKS], lm[:, 0:NKS], ACT.Exp, bias=nmax[:, 0:1],
                                                   accum_out=psums[:, 0:1])
                    ins.then_inc(exp_done, 1)

                def unit_tick(t):
                    if 0 <= t - 2 < NUNITS:
                        attn_copy(t - 2)
                    if 0 <= t - 1 < NUNITS:
                        pt_copy(t - 1)
                    if 0 <= t < NUNITS:
                        exp(t)

                for j in range(12):
                    unit_tick(j - 2)
                    n = first["gates", l] + j
                    chunk_wait(n)
                    nc.scalar.activation(gates[:, 2 * j, :], pair(n, 0), ACT.Sigmoid)
                    nc.scalar.activation(gates[:, 2 * j + 1, :], pair(n, 1), ACT.Sigmoid).then_inc(pair_evac, 1)
                for j in range(4):
                    unit_tick(10 + j)
                    to_tmp(first["short", l] + j, tmp_before["short", l] + j, ACT.Copy, ACT.Copy)

                for j in range(4):
                    if j == 0:
                        act.wait_ge(xc_ready, l + 1)
                        nc.scalar.activation(hT[:, BC:2 * BC, :], hT[:, 0:BC, :], ACT.Square).then_inc(ln_sq, 1)
                    to_tmp(first["attn", l] + j, tmp_before["attn", l] + j, ACT.Copy, ACT.Copy)
                    if j == 0:
                        act.wait_ge(ln_ms, l + 1)
                        nc.scalar.activation(std[:], var[:], ACT.Sqrt).then_inc(ln_std, 1)
                act.wait_ge(ln_n, l + 1)
                for c in range(BC):
                    ins = nc.scalar.activation(confT[:, c, :], hT[:, c, :], ACT.Silu,
                                               scale=vec[:, l, R_LNG + c:R_LNG + c + 1],
                                               bias=vec[:, l, R_LNB + c:R_LNB + c + 1]).then_inc(conf_ready, 1)

                def high(k, it=None):
                    size = SLOT if k < FC else EC * P
                    split_high(first["ffn_in", l] + k, k, wd_hi[:, k % 2, 0:size], size, it, SLOTS)

                for stage in ("conf", "out"):
                    for j in range(4):
                        if stage == "out" and j >= 1:
                            square(2 * l + 1, j - 1)
                        if stage == "out" and j == 3 and l % 2 == 0:
                            high(0)
                            high(1)
                        to_tmp(first[stage, l] + j, tmp_before[stage, l] + j, ACT.Copy, ACT.Copy)

                if l % 2 == 0:
                    n0, t0 = first["ffn_in", l], tmp_before["ffn_in", l]
                    norm(2 * l + 1, gain_of(1), shift_of(1), pairs=(3,))

                    def ffn_in(k, it=None):
                        to_tmp(n0 + k, t0 + k, ACT.Silu, ACT.Copy, it, split=True)
                        high(k + 2, it)

                    with act.Fori(0, FC // SLOTS) as it:
                        for k in range(SLOTS):
                            ffn_in(k, it)
                    for k in range(FC - FC % SLOTS, FC):
                        ffn_in(k)

                    def ffn_out(k, it=None):
                        n, o = first["ffn_out", l] + k, k // 2
                        act.wait_ge(chunk_done, n + 1 if it is None else it * SLOTS + (n + 1))
                        if k % 2:
                            t = tmp_before["ffn_out", l] + o
                            act.wait_ge(tmp_free, t - 1 if it is None else it * (SLOTS // 2) + (t - 1))
                            copy(tmp[:, t % 2, 0, :], mmp[:, 2 * ((o + first["ffn_out", l]) % 2), 0:T]).then_inc(tmp_ready, 1)
                            act.wait_ge(tmp_ready, t + 1 if it is None else it * (SLOTS // 2) + (t + 1))
                        act.sem_inc(pair_evac, 1)
                        if it is not None or k + 2 < 2 * DC:
                            high(FC + k + 2, it)

                    with act.Fori(0, 2 * DC // SLOTS - 1) as it:
                        for k in range(SLOTS):
                            ffn_out(k, it)
                    for k in range(2 * DC - SLOTS, 2 * DC):
                        ffn_out(k)
                else:
                    norm(2 * l + 1, gain_of(1), shift_of(1), pairs=(3,))
                    act.wait_ge(rt_d, 1)
                    nc.scalar.activation(rsc[:, 3:6], rsc[:, 0:3], ACT.Exp).then_inc(rt_e, 1)
                    act.wait_ge(stored, 16 * 10 * DEPTH)
                    for b in range(6):
                        t, g = b // 2, b % 2
                        m = P if t < 2 else TS
                        act.wait_ge(ht_tr, b + 1)
                        copy(h_tok[0:m, t, g * 512:(g + 1) * 512], mmp[0:m, b % 4, :]).then_inc(ht_copied, 1)

                    act.wait_ge(passes_ready, 1)
                    total = act.value_load(pass_i[0:1, NP + 1:NP + 2], min_val=5, max_val=NP)

                    def gathered():
                        copy(xg_hi[:], lg[:, :].rearrange("p (c s) -> p c s", c=DC)).then_inc(xg_ready, 1)

                    def hid_copy(b):
                        w = min(4, EC - 4 * b)
                        copy(hidT_hi[:, 4 * b:4 * b + w, :],
                             (px, py, px)[b][:, 0:w * P].rearrange("p (f s) -> p f s", f=w)).then_inc(hidT_ready, 1)

                    n0, S0 = first["moe", l], FC + 2 * DC
                    sizes = [4 * w for w in GW for _ in range(4)] + [(b - a) * D for a, b in zip(OUT_AT, OUT_AT[1:])]

                    def high(k, p=None):
                        kk = k % CPP
                        fills = CPP // SLOTS
                        n = n0 + kk
                        full = 32 * (n // SLOTS + 1) + (32 * fills if k >= CPP else 0)
                        if p is None:
                            act.wait_ge(w_full[n % SLOTS], full)
                        else:
                            act.wait_ge(w_full[n % SLOTS], p * (32 * fills) + full)
                            act.wait_ge(chunk_done, p * CPP + (n0 + k - AHEAD + 1))
                        copy(we_hi[:, k % AHEAD, 0:sizes[kk]], ring_flat(n, sizes[kk])).then_inc(hi_ready, 1)

                    for k in range(AHEAD):
                        if k == AHEAD - 1:
                            act.wait_ge(xg_done, 1)
                            gathered()
                        high(k)
                    with act.Fori(0, total) as p:
                        for k in range(CPP):
                            act.wait_ge(chunk_done, p * CPP + (n0 + k + 1))
                            if k in (1, 5, 9):
                                g = k // 4
                                w = GW[g]
                                nc.scalar.activation(hid_tok[:, 512 * g:512 * g + w], mmp[:, 2 * (g % 2), 0:w],
                                                     ACT.Silu).then_inc(silu_ready, 1)
                            if k == 8:
                                act.wait_ge(st2_tr, p + 1)
                                copy(ST[:], py[:, 0:T])
                                copy(wslot[:], px[:, 0:1]).then_inc(st2_ready, 1)
                            if k == 10:
                                for b in range(2):
                                    act.wait_ge(hid_tr, p * 3 + (b + 1))
                                    hid_copy(b)
                            if k == 14:
                                act.wait_ge(hid_tr, p * 3 + 3)
                                hid_copy(2)
                            if k == 16:
                                act.wait_ge(xg_done, p + 2)
                                gathered()
                            if k == CPP - 1:
                                act.wait_ge(st2_ready, p + 1)
                                for h in range(2):
                                    ins = nc.scalar.activation(y[:, h * 512:(h + 1) * 512], mmp[:, 2 + h, :],
                                                               ACT.Copy, scale=wslot[:, 0:1])
                                ins.then_inc(yslot_ready, 1)
                            high(k + AHEAD, p)

            norm(4, lambda c: vec[:, 0, R_GFIN + c:R_GFIN + c + 1], lambda c: None)
            for t in range(3):
                act.wait_ge(y_copied, 2 * (t + 1))
                if t < 2:
                    act.dma_start(y_prompt[0, t * P:(t + 1) * P, :], x_tok[:, t, :]).then_inc(y_stored, 16)
                else:
                    act.dma_start(y_sample[0], x_tok[0:TS, t, :]).then_inc(y_stored, 16)
            act.wait_ge(y_stored, 48)
            act.wait_ge(stored, 16 * 10 * DEPTH)

        @block.vector
        def _(dve):
            V = nc.vector
            steps = [0]

            def link(ins):
                steps[0] += 1
                ins.then_inc(dve_step, 1)
                dve.wait_ge(dve_step, steps[0])

            b = 0

            def pro(dst, src):
                nonlocal b
                dve.wait_ge(pro_tr, b + 1)
                if not isinstance(dst, list):
                    dst, src = [dst], [src]
                for i, (d, s) in enumerate(zip(dst, src)):
                    ins = V.tensor_copy(d, s(mmp[:, b % 4, :]))
                ins.then_inc(pro_copied, 1)
                b += 1

            for l in range(DEPTH):
                dve.wait_ge(pro_tr, b + 1)
                link(V.tensor_copy(vec[:, l, :], mmp[:, b % 4, 0:NROWS]))
                V.tensor_copy(dwc[:, l, :], mmp[:, b % 4, P:P + CW * BC]).then_inc(pro_copied, 1)
                b += 1
            def pro_rest():
                for t in range(3):
                    m = P if t < 2 else TS
                    for g in range(2):
                        pro(xT[:, 4 * g:4 * g + 4, t * P:t * P + m],
                            lambda s: s.rearrange("p (j t) -> p j t", j=4)[:, :, 0:m])
                for l in range(DEPTH):
                    for dst in (kTs, ikTs):
                        pro(dst[:, l, 0:PAST], lambda s: s)
                    pro(hist[:, l, :, :], lambda s: s[:, 0:P].rearrange("p (j t) -> p j t", j=4))

            for l in range(DEPTH):
                if l == 1:
                    pro_rest()
                    dve.wait_ge(pro_copied, 14)
                    dve.sem_inc(x_ready, DC // 2)
                for g3 in range(3):
                    dve.wait_ge(mod_tr, 3 * l + g3 + 1)
                    bank = (lg[:, 0:512], lg[:, 512:1024], px)[g3].rearrange("p (q g w) -> p q g w", q=4, g=4)
                    for q in range(4):
                        i, h = (4 * g3 + q) // 2, q % 2
                        j = slice(8 * i + h, 8 * i + h + 7, 2)
                        ins = V.tensor_tensor(mods[:, l, j, :], bank[:, q, :, 0:2],
                                              vec[:, l, R_BADA:R_BADA + 48][:, j].unsqueeze(2).broadcast_to([P, 4, 2]),
                                              ALU.add)
                link(ins)
                for w, r in ((0, R_GMIX), (1, R_GFFN)):
                    link(V.tensor_scalar(gain[:, l, w, :, :], mods[:, l, 24 * w + 8:24 * w + 16, :], 1.0, None, ALU.add))
                    link(V.tensor_tensor(gain[:, l, w, :, :], gain[:, l, w, :, :],
                                         vec[:, l, r:r + 8].unsqueeze(2).broadcast_to([P, DC, 2]), ALU.mult))
                dve.sem_inc(mods_ready, 1)

            def norm(k):
                dve.wait_ge(sum_ready, k + 1)
                V.tensor_scalar(var[:], py[:, 0:T], 1.0 / D, EPS, ALU.mult, ALU.add).then_inc(ms_ready, 1)
                dve.wait_ge(std_ready, k + 1)
                link(V.reciprocal(rstd[:], std[:]))
                for c in range(DC + 1):
                    if c < DC:
                        V.tensor_tensor(hT[:, c, :], xT[:, c, :], rstd[:], ALU.mult).then_inc(xn_step, 1)
                    if c > 0:
                        dve.wait_ge(xn_step, DC * k + c)
                        j, cols = c - 1, hT[:, c - 1, TP:T]
                        if k == 2 * DEPTH:
                            ins = V.tensor_scalar(cols, cols, vec[:, 0, R_GFIN + j:R_GFIN + j + 1], None, ALU.mult)
                        else:
                            ins = V.tensor_scalar(cols, cols, gain[:, k // 2, k % 2, j, 1:2],
                                                  mods[:, k // 2, 24 * (k % 2) + j, 1:2], ALU.mult, ALU.add)
                        ins.then_inc(xn_ready, 1)

            def bcast(ap, n, w):
                return ap.unsqueeze(1).broadcast_to([P, n, w])

            score_areas = ((0, P, TOPK_P), (P, P + TP, TOPK_P), (P + TP, 960, TOPK_S))

            for l in range(DEPTH):
                norm(2 * l)

                dve.wait_ge(kv_copied, 3 * (l + 1))
                link(V.tensor_scalar(iws[:], kvtok[:, :, 2 * P + HD:2 * P + HD + NH], NH ** -0.5, None, ALU.mult))
                for h in range(NH):
                    dve.wait_ge(rel_ready, 8 * l + h + 1)
                    for t, (a, z, _) in enumerate(score_areas):
                        w = iws[:, t, h:h + 1]
                        if h == 0:
                            ins = V.tensor_scalar(score[:, a:z], rel[:, 0, a:z], w, None, ALU.mult)
                        else:
                            ins = V.scalar_tensor_tensor(score[:, a:z], rel[:, h % 2, a:z], w, score[:, a:z],
                                                         ALU.mult, ALU.add)
                    ins.then_inc(rel_used, 1)
                    dve.wait_ge(rel_used, 8 * l + h + 1)

                link(V.memset(score[0:CHUNK, CHUNK:P], INADMISSIBLE))
                link(V.memset(score[0:CHUNK, P + TP - CHUNK:P + TP], INADMISSIBLE))

                for a, z, k in score_areas:
                    for r in range(k // 8):
                        src = score if r == 0 else work
                        link(V.max(out=top8[:], in_=src[:, a:z]))
                        link(V.match_replace(out=work[:, a:z], in_to_replace=top8[:], in_values=src[:, a:z],
                                             imm_value=TAKEN))
                    link(V.tensor_scalar(score[:, a:z], work[:, a:z], TAKEN, NEG_MASK, ALU.is_gt, ALU.mult))
                mask = score

                dve.wait_ge(u_ready, 8 * (l + 1))
                dve.wait_ge(hist_ready, l + 1)
                w_sh = USW - SH
                for w in range(SW):
                    for c in range(BC):
                        tap = vec[:, l, R_WSH + 4 * w + c:R_WSH + 4 * w + c + 1]
                        src = u_short[:, c, w:w + w_sh]
                        if w == 0:
                            ins = V.tensor_scalar(sconv[:, c, :], src, tap, None, ALU.mult)
                        else:
                            ins = V.scalar_tensor_tensor(sconv[:, c, :], src, tap, sconv[:, c, :], ALU.mult, ALU.add)
                    link(ins)
                dve.wait_ge(pair_evac, first["bgate", l] + 2 - ADA_CHUNKS)
                dve.wait_ge(st_tr, 4 * (l + 1))
                for src, ts in segs(sconv, 0, US_S - SH):
                    link(V.tensor_tensor(shortT[:, :, ts], src, bgate[:, :, ts], ALU.mult))
                dve.sem_inc(short_ready, 1)

                taps = [(w, c) for w in range(CW) for c in range(BC)]
                w_cv = UCW - CH

                def conv_taps(count):
                    for w, c in taps[:count]:
                        tap = dwc[:, l, w * BC + c:w * BC + c + 1]
                        src = u_conf[:, c, w:w + w_cv]
                        if w == 0:
                            ins = V.tensor_scalar(conv[:, c, :], src, tap, vec[:, l, R_BDW + c:R_BDW + c + 1],
                                                  ALU.mult, ALU.add)
                        else:
                            ins = V.scalar_tensor_tensor(conv[:, c, :], src, tap, conv[:, c, :], ALU.mult, ALU.add)
                        if c == BC - 1:
                            link(ins)
                    del taps[:count]

                for u in range(NUNITS):
                    g = NUNITS * l + u
                    dve.wait_ge(lg_done, g + 1)
                    if u < 8:
                        keys = P * (u // 4 + 1)
                        a = 0 if u < 4 else P
                        v3 = lm[:, 0:2 * keys].rearrange("p (h k) -> p h k", h=2)
                        link(V.scalar_tensor_tensor(v3, lg[:, :].rearrange("p (h k) -> p h k", h=2)[:, :, 0:keys],
                                                    HD ** -0.5, bcast(mask[:, a:a + keys], 2, keys),
                                                    ALU.mult, ALU.add))
                        V.tensor_reduce(nmax[:, 0:2], v3, AX, ALU.max, negate=True).then_inc(lm_done, 1)
                    else:
                        link(V.scalar_tensor_tensor(lm[:], lg[:, 0:NKS], HD ** -0.5, mask[:, P + TP:960],
                                                    ALU.mult, ALU.add))
                        V.tensor_reduce(nmax[:, 0:1], lm[:], AX, ALU.max, negate=True).then_inc(lm_done, 1)
                    conv_taps(10)
                    dve.wait_ge(exp_done, g + 1)
                    if u < 8:
                        link(V.reciprocal(prec[:], psums[:]))
                        v3 = prob[:, 0:2 * keys].rearrange("p (h k) -> p h k", h=2)
                        V.tensor_tensor(v3, v3, prec[:].unsqueeze(2).broadcast_to([P, 2, keys]),
                                        ALU.mult).then_inc(prob_ready, 1)
                    else:
                        link(V.reciprocal(prec[:, 0:1], psums[:, 0:1]))
                        V.tensor_scalar(prob[:], prob[:], prec[:, 0:1], None, ALU.mult).then_inc(prob_ready, 1)
                conv_taps(len(taps))
                dve.sem_inc(conv_ready, 1)

                def merge(stage, j, gate0, is_first):
                    t = tmp_before[stage, l] + j
                    dve.wait_ge(tmp_ready, t + 1)
                    both = tmp[:, t % 2, :, :]
                    g_ap = gates[:, gate0 + 2 * j:gate0 + 2 * j + 2, :]
                    dst = merged[:, 2 * j:2 * j + 2, :]
                    if is_first:
                        V.tensor_tensor(dst, both, g_ap, ALU.mult).then_inc(tmp_free, 1)
                        dve.wait_ge(tmp_free, t + 1)
                    else:
                        link(V.tensor_tensor(both, both, g_ap, ALU.mult))
                        V.tensor_tensor(dst, dst, both, ALU.add).then_inc(tmp_free, 1)
                        dve.wait_ge(tmp_free, t + 1)

                dve.wait_ge(tmp_free, tmp_before["short", l])
                for j in range(4):
                    merge("short", j, 2 * DC, True)
                for j in range(4):
                    if j == 0:
                        dve.wait_ge(ln_sum, l + 1)
                        link(V.tensor_scalar(mean[:], px[:, 0:T], 1.0 / DB, None, ALU.mult))
                        for src, ts in segs(conv, 0, UC_S - CH):
                            ins = V.tensor_tensor(hT[:, 0:BC, ts], src, bcast(mean[:, ts], BC, ts.stop - ts.start),
                                                  ALU.subtract)
                            link(ins)
                        dve.sem_inc(xc_ready, 1)
                    merge("attn", j, 0, False)
                    if j == 0:
                        dve.wait_ge(ln_ss, l + 1)
                        V.tensor_scalar(var[:], py[:, 0:T], 1.0 / DB, EPS, ALU.mult, ALU.add).then_inc(ln_ms, 1)
                        dve.wait_ge(ln_std, l + 1)
                        link(V.reciprocal(rstd[:], std[:]))
                        V.tensor_tensor(hT[:, 0:BC, :], hT[:, 0:BC, :], bcast(rstd[:], BC, T),
                                        ALU.mult).then_inc(ln_n, 1)
                for j in range(4):
                    merge("conf", j, DC, False)
                    dve.sem_inc(merged_ready, 1)

                def add_to_x(j, src, which):
                    for s, ts in enumerate((slice(0, TP), slice(TP, T))):
                        ins = V.scalar_tensor_tensor(xT[:, j, ts], src[:, ts], mods[:, l, 24 * which + 16 + j, s:s + 1],
                                                     xT[:, j, ts], ALU.mult, ALU.add)
                    return ins

                def low(k, it=None):
                    n = first["ffn_in", l] + k
                    size = SLOT if k < FC else EC * P
                    dve.wait_ge(hi_ready, k + 1 if it is None else it * SLOTS + (k + 1))
                    V.tensor_tensor(wd_lo[:, k % 2, 0:size], ring[:, n % SLOTS, 0:size],
                                    wd_hi[:, k % 2, 0:size].bitcast(F32), ALU.subtract).then_inc(lo_ready, 1)
                    dve.wait_ge(lo_ready, k + 1 if it is None else it * SLOTS + (k + 1))
                    dve.sem_inc(slot_free[n % SLOTS], 1)

                for j in range(4):
                    if j == 3 and l % 2 == 0:
                        low(0)
                        low(1)
                    t = tmp_before["out", l] + j
                    dve.wait_ge(tmp_ready, t + 1)
                    add_to_x(2 * j, tmp[:, t % 2, 0, :], 0)
                    add_to_x(2 * j + 1, tmp[:, t % 2, 1, :], 0).then_inc(tmp_free, 1)
                    dve.wait_ge(tmp_free, t + 1)
                    dve.sem_inc(x_ready, 1)

                if l % 2 == 0:
                    n0, t0 = first["ffn_in", l], tmp_before["ffn_in", l]

                    norm(2 * l + 1)
                    for c in range(DC):
                        dve.wait_ge(h_ready, DC * (2 * l + 1) + c + 1)
                        link(V.tensor_copy(h_hi[:, c, :], hT[:, c, :]))
                        V.tensor_tensor(h_lo[:, c, :], hT[:, c, :], h_hi[:, c, :].bitcast(F32),
                                        ALU.subtract).then_inc(hl_ready, 1)

                    def gate_up(k, it=None):
                        t = t0 + k
                        dve.wait_ge(tmp_ready, t + 1 if it is None else it * SLOTS + (t + 1))
                        V.tensor_tensor(hidf[:, k % 2, :], tmp[:, t % 2, 0, :], tmp[:, t % 2, 1, :],
                                        ALU.mult).then_inc(tmp_free, 1)
                        dve.wait_ge(tmp_free, t + 1 if it is None else it * SLOTS + (t + 1))
                        if it is None:
                            hi, lo = hid_hi[:, k, :], hid_lo[:, k, :]
                        else:
                            hi, lo = (x[:, bass.ds(it * SLOTS + k, 1), :].rearrange("p a t -> p (a t)")
                                      for x in (hid_hi, hid_lo))
                        V.tensor_copy(hi, hidf[:, k % 2, :]).then_inc(hid_step, 1)
                        dve.wait_ge(hid_step, k + 1 if it is None else it * SLOTS + (k + 1))
                        V.tensor_tensor(lo, hidf[:, k % 2, :], hi.bitcast(F32), ALU.subtract).then_inc(hid_ready, 1)
                        low(k + 2, it)

                    with dve.Fori(0, FC // SLOTS) as it:
                        for k in range(SLOTS):
                            gate_up(k, it)
                    for k in range(FC - FC % SLOTS, FC):
                        gate_up(k)
                    t0 = tmp_before["ffn_out", l]
                    for k in range(2 * DC):
                        if k % 2:
                            o = k // 2
                            dve.wait_ge(tmp_ready, t0 + o + 1)
                            add_to_x(o, tmp[:, (t0 + o) % 2, 0, :], 1).then_inc(tmp_free, 1)
                            if o % 2:
                                dve.wait_ge(tmp_free, t0 + o + 1)
                                dve.sem_inc(x_ready, 1)
                        if k + 2 < 2 * DC:
                            low(FC + k + 2)
                else:
                    norm(2 * l + 1)
                    dve.wait_ge(rt_done, 1)
                    link(V.memset(small[:], 0.0))
                    link(V.memset(rsc[:], 0.0))
                    for t in range(3):
                        m = P if t < 2 else TS
                        link(V.tensor_copy(rl[0:m, t, :], px[0:m, t * NE:(t + 1) * NE]))
                        link(V.max(out=top8[0:m, :], in_=rl[0:m, t, :]))
                        link(V.max_index(out=idx_u[0:m, :], in_max=top8[0:m, :], in_values=rl[0:m, t, :]))
                        link(V.tensor_copy(idx_f[0:m, 2 * t:2 * t + 2], idx_u[0:m, 0:2]))
                        link(V.tensor_tensor(rsc[0:m, t:t + 1], top8[0:m, 1:2], top8[0:m, 0:1], ALU.subtract))
                    dve.sem_inc(rt_d, 1)
                    iota8 = iota_f[:, 0:NE]
                    for t in range(3):
                        m = P if t < 2 else TS
                        link(V.tensor_scalar(member[0:m, t, :], iota8[0:m, :], idx_f[0:m, 2 * t:2 * t + 1], None,
                                             ALU.is_equal))
                        link(V.tensor_scalar(comb2[0:m, :], iota8[0:m, :], idx_f[0:m, 2 * t + 1:2 * t + 2], None,
                                             ALU.is_equal))
                        link(V.tensor_tensor(member[0:m, t, :], member[0:m, t, :], comb2[0:m, :], ALU.add))
                    dve.sem_inc(comb_ready, 1)
                    dve.wait_ge(rt_e, 1)
                    link(V.memset(comb[:], 0.0))
                    link(V.tensor_scalar(rsc[:, 0:3], rsc[:, 3:6], 1.0, None, ALU.add))
                    link(V.reciprocal(rsc[:, 0:3], rsc[:, 0:3]))
                    link(V.tensor_tensor(rsc[:, 3:6], rsc[:, 3:6], rsc[:, 0:3], ALU.mult))
                    for t in range(3):
                        m = P if t < 2 else TS
                        link(V.tensor_scalar(comb[0:m, t, :], iota8[0:m, :], idx_f[0:m, 2 * t:2 * t + 1],
                                             rsc[0:m, t:t + 1], ALU.is_equal, ALU.mult))
                        link(V.tensor_scalar(comb2[0:m, :], iota8[0:m, :], idx_f[0:m, 2 * t + 1:2 * t + 2],
                                             rsc[0:m, 3 + t:4 + t], ALU.is_equal, ALU.mult))
                        link(V.tensor_tensor(comb[0:m, t, :], comb[0:m, t, :], comb2[0:m, :], ALU.add))

                    dve.wait_ge(rank_done, 1)
                    link(V.tensor_copy(rank, py[:, 0:3 * NE].rearrange("p (t e) -> p t e", t=3)))
                    link(V.tensor_copy(count, py[:, 3 * NE:4 * NE]))
                    link(V.tensor_scalar(npass, count, 0.5, None, ALU.is_gt))
                    for more in range(1, (T + P - 1) // P):
                        link(V.tensor_scalar(cum, count, P * more + 0.5, None, ALU.is_gt))
                        link(V.tensor_tensor(npass, npass, cum, ALU.add))
                    link(V.tensor_tensor_scan(cum, ones[:, 0:NE], npass, 0.0, ALU.mult, ALU.add))
                    pass_no = iota_f[:, 0:NPT]

                    def over_e(ap):
                        return ap.unsqueeze(2).broadcast_to([P, NPT, NE])

                    def over_p(ap):
                        return ap.unsqueeze(1).broadcast_to([P, NPT, NE])

                    link(V.tensor_tensor(ended, over_p(cum), over_e(pass_no), ALU.is_le))
                    link(V.tensor_reduce(pass_e, ended, AX, ALU.add))
                    link(V.tensor_tensor(picked, ended, over_p(npass), ALU.mult))
                    link(V.tensor_reduce(pass_start, picked, AX, ALU.add))
                    link(V.tensor_tensor(pass_base, pass_no, pass_start, ALU.subtract))
                    link(V.tensor_scalar(pass_base, pass_base, float(P), -1.0, ALU.mult, ALU.add))
                    link(V.tensor_copy(pass_i[:, 0:NPT], pass_e))
                    link(V.tensor_copy(pass_i[:, NPT:NPT + 1], cum[:, NE - 1:NE]))
                    dve.sem_inc(passes_ready, 1)
                    link(V.tensor_tensor(picked, over_p(iota8), over_e(pass_e), ALU.is_equal))
                    for dst, src in ((row_rank, rank), (row_in, member), (row_w, comb)):
                        for t in range(3):
                            link(V.tensor_tensor(prod[:, t], picked, over_p(src[:, t, :]), ALU.mult))
                        link(V.tensor_reduce(dst, prod, AX, ALU.add))
                    base3 = pass_base.unsqueeze(1).broadcast_to([P, 3, NPT])
                    link(V.tensor_tensor(row_rank, row_rank, base3, ALU.subtract))
                    link(V.tensor_tensor(row_rank, row_rank, row_in, ALU.mult))
                    link(V.tensor_scalar(row_rank, row_rank, -1.0, None, ALU.add))
                    dve.sem_inc(tables_ready, 1)
                    total = dve.value_load(pass_i[0:1, NP + 1:NP + 2], min_val=5, max_val=NP)

                    def select_slots(p):
                        for t in range(3):
                            r = row_rank[:, t, 0:1] if p is None else row_rank[:, t, bass.ds(p + 1, 1)]
                            ins = V.tensor_scalar(S[:, t, :], iota_f[:], r, None, ALU.is_equal)
                        ins.then_inc(s_ready, 1)

                    select_slots(None)
                    link(V.memset(ST[:], 0.0))
                    V.memset(y[:], 0.0).then_inc(yslot_ready, 1)
                    dve.wait_ge(acc_zeroed, 1)

                    def add_scattered(c, done):
                        bank = (lg[:, 0:T], lg[:, 512:512 + T], px[:, 0:T], py[:, 0:T])[c % 4]
                        dve.wait_ge(sc2_done, done + (c + 1))
                        V.tensor_tensor(acc[:, c, :], acc[:, c, :], bank, ALU.add).then_inc(sc2_added, 1)

                    n0, S0 = first["moe", l], FC + 2 * DC
                    sizes = [4 * w for w in GW for _ in range(4)] + [(b - a) * D for a, b in zip(OUT_AT, OUT_AT[1:])]

                    def low(k, p=None):
                        size, u = sizes[k % CPP], k % AHEAD
                        count = S0 + k + 1
                        dve.wait_ge(hi_ready, count if p is None else p * CPP + count)
                        V.tensor_tensor(we_lo[:, u, 0:size], ring[:, (n0 + k % CPP) % SLOTS, 0:size],
                                        we_hi[:, u, 0:size].bitcast(F32), ALU.subtract).then_inc(lo_ready, 1)
                        dve.wait_ge(lo_ready, count if p is None else p * CPP + count)
                        dve.sem_inc(slot_free[(n0 + k % CPP) % SLOTS], 1)

                    def low_gathered(count):
                        dve.wait_ge(xg_ready, count)
                        V.tensor_tensor(xg_lo[:], lg[:, :].rearrange("p (c s) -> p c s", c=DC), xg_hi[:].bitcast(F32),
                                        ALU.subtract).then_inc(xg_split, 1)

                    def low_hid(b, count):
                        w = min(4, EC - 4 * b)
                        dve.wait_ge(hidT_ready, count)
                        V.tensor_tensor(hidT_lo[:, 4 * b:4 * b + w, :],
                                        (px, py, px)[b][:, 0:w * P].rearrange("p (f s) -> p f s", f=w),
                                        hidT_hi[:, 4 * b:4 * b + w, :].bitcast(F32),
                                        ALU.subtract).then_inc(hidT_split, 1)

                    for k in range(AHEAD):
                        if k == AHEAD - 1:
                            low_gathered(1)
                        low(k)
                    with dve.Fori(0, total) as p:
                        for k in range(CPP):
                            if 3 <= k < 7:
                                add_scattered(2 * (k - 3), p * DC)
                                add_scattered(2 * (k - 3) + 1, p * DC)
                            if k in (3, 7, 11):
                                g = k // 4
                                dve.wait_ge(chunk_done, p * CPP + (n0 + k + 1))
                                dve.wait_ge(silu_ready, p * 3 + (g + 1))
                                h = hid_tok[:, 512 * g:512 * g + GW[g]]
                                V.tensor_tensor(h, h, mmp[:, 2 * (g % 2) + 1, 0:GW[g]], ALU.mult).then_inc(hg_ready, 1)
                            if k == 8:
                                dve.wait_ge(st2_tr, p + 1)
                                select_slots(p)
                            if k == 10:
                                for b in range(2):
                                    low_hid(b, p * 3 + (b + 1))
                            if k == 14:
                                low_hid(2, p * 3 + 3)
                            if k == 16:
                                low_gathered(p + 2)
                            low(k + AHEAD, p)
                    for c in range(DC):
                        add_scattered(c, total * DC)
                        dve.wait_ge(sc2_added, total * DC + (c + 1))
                        ins = add_to_x(c, acc[:, c, :], 1)
                        if c % 2:
                            link(ins)
                            dve.sem_inc(x_ready, 1)

            norm(4)
            for b in range(6):
                t, g = b // 2, b % 2
                m = P if t < 2 else TS
                dve.wait_ge(y_tr, b + 1)
                V.tensor_copy(x_tok[0:m, t, g * 512:(g + 1) * 512], mmp[0:m, b % 4, :]).then_inc(y_copied, 1)


_INS = ['x_prompt', 'x_sample', 'cache_k', 'cache_v', 'cache_idx_k', 'state_conv_conformer', 'state_conv_short',
        'c_prompt', 'c_sample', 'w_ada', 'b_ada', 'g_norm_mix', 'g_norm_ffn', 'w_in', 'w_dw_conf', 'b_dw_conf',
        'ln_conf_g', 'ln_conf_b', 'w_dw_short', 'w_branch', 'w_out', 'w_ffn_in', 'w_ffn_out', 'w_router', 'b_router',
        'w_exp_in', 'w_exp_out', 'g_final']
_OUTS = [(1, TP, D), (1, TS, D),
         (DEPTH, 1, TP, HD), (DEPTH, 1, TP, HD), (DEPTH, 1, TP, HD), (DEPTH, 1, CH, DB), (DEPTH, 1, SH, DB),
         (DEPTH, 1, TS, HD), (DEPTH, 1, TS, HD), (DEPTH, 1, TS, HD), (DEPTH, 1, CH, DB), (DEPTH, 1, SH, DB)]


def kernel(**inputs):
    import numpy as _np
    import concourse.bacc as _bacc
    from concourse import mybir as _mybir
    from concourse.bass_utils import run_bass_kernel_spmd as _run

    nc = _bacc.Bacc("TRN2", target_bir_lowering=False, num_devices=1)
    arrays, args = {}, []
    for name in _INS:
        a = _np.ascontiguousarray(inputs[name])
        arrays[f"in_{name}_dram"] = a
        args.append(nc.dram_tensor(f"in_{name}_dram", a.shape, _mybir.dt.from_np(a.dtype), kind="ExternalInput").ap())
    for i, shape in enumerate(_OUTS):
        args.append(nc.dram_tensor(f"out_{i}_dram", shape, _mybir.dt.float32, kind="ExternalOutput").ap())
    build(nc, *args)
    r = _run(nc, [arrays], core_ids=[0])
    return tuple(r.results[0][f"out_{i}_dram"] for i in range(len(_OUTS)))
```
